# Optimizing a Trainium2 kernel written in Bass

```python
import math
import jax, jax.numpy as jnp
from jax import lax
import numpy as np

D_MODEL = 1024
BATCH = 1
SEQ = 512
DEPTH = 2

N_A = DEPTH // 2
N_B = DEPTH - N_A
N_HEADS = 16
HEAD_DIM = D_MODEL // N_HEADS
D_FF = 4 * D_MODEL
CONV_W = 3
Q_BLOCK = 128
N_MOD = 6
EPS = 1e-6

kernel_name = "yoco_shortconv_fox_adaln_trunk"

def rms_norm(x, g):
    xf = x.astype(jnp.float32)
    y = xf * lax.rsqrt(jnp.mean(xf * xf, axis=-1, keepdims=True) + EPS)
    return y.astype(x.dtype) * g

def modulate(h, shift, scale):
    return h * (1 + scale[:, None, :]) + shift[:, None, :]

def short_conv_mixer(h, w_in, conv_w, w_out):
    d = h.shape[-1]
    u = h @ w_in
    b_g, c_g, xv = jnp.split(u, 3, axis=-1)
    z = c_g * xv
    zc = lax.conv_general_dilated(
        z, conv_w[:, None, :],
        window_strides=(1,), padding=[(CONV_W - 1, 0)],
        dimension_numbers=("NWC", "WIO", "NWC"),
        feature_group_count=d)
    return (b_g * zc) @ w_out

def squared_relu_mlp(h, w1, w2):
    a = jax.nn.relu(h @ w1)
    return (a * a) @ w2

def shared_kv(x, kv_norm_g, w_kv, k_norm_g, w_f, b_f):
    b, s, d = x.shape
    h = rms_norm(x, kv_norm_g)
    k, v = jnp.split(h @ w_kv, 2, axis=-1)
    k = rms_norm(k.reshape(b, s, N_HEADS, HEAD_DIM), k_norm_g)
    v = v.reshape(b, s, N_HEADS, HEAD_DIM)
    log_f = jax.nn.log_sigmoid((h @ w_f + b_f).astype(jnp.float32))
    F = jnp.cumsum(log_f, axis=1)
    return k, v, jnp.transpose(F, (0, 2, 1))

def fox_mixer(h, q_w, q_norm_g, o_w, k, v, F):
    b, s, d = h.shape
    nblk = s // Q_BLOCK
    q = rms_norm((h @ q_w).reshape(b, s, N_HEADS, HEAD_DIM), q_norm_g)
    q_blocks = q.reshape(b, nblk, Q_BLOCK, N_HEADS, HEAD_DIM).transpose(1, 0, 2, 3, 4)
    F_blocks = F.reshape(b, N_HEADS, nblk, Q_BLOCK).transpose(2, 0, 1, 3)
    offsets = jnp.arange(nblk, dtype=jnp.int32) * Q_BLOCK
    key_pos = jnp.arange(s, dtype=jnp.int32)
    scale = 1.0 / math.sqrt(HEAD_DIM)

    def one_block(args):
        qb, Fq, off = args
        logits = jnp.einsum("bqhd,bkhd->bhqk", qb, k).astype(jnp.float32) * scale
        logits = logits + (Fq[..., :, None] - F[..., None, :])
        q_pos = off + jnp.arange(Q_BLOCK, dtype=jnp.int32)
        causal = key_pos[None, :] <= q_pos[:, None]
        logits = jnp.where(causal[None, None], logits, -1e30)
        p = jax.nn.softmax(logits, axis=-1)
        return jnp.einsum("bhqk,bkhd->bqhd", p.astype(v.dtype), v)

    out = lax.map(one_block, (q_blocks, F_blocks, offsets))
    out = out.transpose(1, 0, 2, 3, 4).reshape(b, s, d)
    return out @ o_w

def setup_inputs(seed: int = 0) -> dict:
    key = jax.random.key(seed)
    ks = jax.random.split(key, 24)
    D, H, hd, FF = D_MODEL, N_HEADS, HEAD_DIM, D_FF
    nrm = lambda k, shape, s: jax.random.normal(k, shape, jnp.float32) * s
    gain = lambda k, shape: 1.0 + 0.05 * jax.random.normal(k, shape, jnp.float32)
    return {
        "x": nrm(ks[0], (BATCH, SEQ, D), 1.0),
        "c": nrm(ks[1], (BATCH, D), 1.0),
        "ada_w": nrm(ks[2], (DEPTH, D, N_MOD * D), 0.5 * D ** -0.5),
        "ada_b": nrm(ks[3], (DEPTH, N_MOD * D), 0.1),
        "norm_mix_g": gain(ks[4], (DEPTH, D)),
        "norm_mlp_g": gain(ks[5], (DEPTH, D)),
        "sc_w_in": nrm(ks[6], (N_A, D, 3 * D), D ** -0.5),
        "sc_conv": nrm(ks[7], (N_A, CONV_W, D), CONV_W ** -0.5),
        "sc_w_out": nrm(ks[8], (N_A, D, D), D ** -0.5),
        "kv_norm_g": gain(ks[9], (D,)),
        "w_kv": nrm(ks[10], (D, 2 * D), D ** -0.5),
        "k_norm_g": gain(ks[11], (hd,)),
        "w_f": nrm(ks[12], (D, H), 0.5 * D ** -0.5),
        "b_f": jax.random.uniform(ks[13], (H,), jnp.float32, 1.0, 6.0),
        "q_w": nrm(ks[14], (N_B, D, D), D ** -0.5),
        "q_norm_g": gain(ks[15], (N_B, hd)),
        "o_w": nrm(ks[16], (N_B, D, D), D ** -0.5),
        "mlp_w1": nrm(ks[17], (DEPTH, D, FF), D ** -0.5),
        "mlp_w2": nrm(ks[18], (DEPTH, FF, D), FF ** -0.5),
    }

def reference(x, c, ada_w, ada_b, norm_mix_g, norm_mlp_g, sc_w_in, sc_conv, sc_w_out,
              kv_norm_g, w_kv, k_norm_g, w_f, b_f, q_w, q_norm_g, o_w, mlp_w1, mlp_w2):
    c_act = jax.nn.silu(c)
    k = v = F = None
    for l in range(DEPTH):
        mod = c_act @ ada_w[l] + ada_b[l]
        sh_m, sc_m, g_m, sh_f, sc_f, g_f = jnp.split(mod, N_MOD, axis=-1)
        h = modulate(rms_norm(x, norm_mix_g[l]), sh_m, sc_m)
        if l < N_A:
            y = short_conv_mixer(h, sc_w_in[l], sc_conv[l], sc_w_out[l])
        else:
            i = l - N_A
            y = fox_mixer(h, q_w[i], q_norm_g[i], o_w[i], k, v, F)
        x = x + g_m[:, None, :] * y
        h = modulate(rms_norm(x, norm_mlp_g[l]), sh_f, sc_f)
        x = x + g_f[:, None, :] * squared_relu_mlp(h, mlp_w1[l], mlp_w2[l])
        if l == N_A - 1:
            k, v, F = shared_kv(x, kv_norm_g, w_kv, k_norm_g, w_f, b_f)
    return x


_drawn_inputs = setup_inputs


def setup_inputs(seed=0):
    import zlib

    import numpy as np

    out = dict(_drawn_inputs(seed))
    spreads = {}
    factors = {'kv_norm_g': 8.0, 'k_norm_g': 8.0, 'w_f': 8.0, 'q_norm_g': 8.0}
    for name, (base, spread) in spreads.items():
        noise = np.random.default_rng([zlib.crc32(name.encode()), seed]).standard_normal(out[name].shape)
        drawn = base * np.exp(spread * noise) if base else spread * noise
        out[name] = __import__('jax').numpy.asarray(drawn.astype(out[name].dtype))
    for name, factor in factors.items():
        out[name] = (out[name] * factor).astype(out[name].dtype)
    return out
```

```python
from contextlib import ExitStack

import concourse.bass as bass
from concourse import mybir

F32 = mybir.dt.float32
F32R = mybir.dt.float32r
BF16 = mybir.dt.bfloat16
ALU = mybir.AluOpType
ACT = mybir.ActivationFunctionType
AX_X = mybir.AxisListType.X

P = 128
D = 1024
T = 512
KT = D // P
TT = T // P
FF = 4 * D
CH = FF // D
HEADS = 16
HD = D // HEADS
CONV = 3
NMOD = 6
EPS = 1e-6
MASKED = -1e30

WIN = 0
WOUT = WIN + 3 * KT
MLP0 = WOUT + KT
KVQ = MLP0 + 2 * CH * KT
OUT = KVQ + 3 * KT
MLP1 = OUT + KT
BLOCKS = MLP1 + 2 * CH * KT
GROUP = 4

KVQ_ORDER = [("k", 0), ("v", 0), ("q", 0)] + [(kind, j) for j in range(1, KT) for kind in "qkv"]
BLOCK_OF = {name: KVQ + n for n, name in enumerate(KVQ_ORDER)}
NORM_ORDER = [name for name in KVQ_ORDER if name[0] != "v"]
NORM_OF = {name: n for n, name in enumerate(NORM_ORDER)}
KVQ_BANK = {"q": 0, "k": 1, "v": 2}
MISC = 3

R_C, R_MIX, R_MLP, R_CONV, R_KV, R_KN, R_QN = 0, 8, 24, 40, 64, 72, 73
ROWS = 74

P_OFF = [P * (qt * (qt + 1) // 2) for qt in range(TT)]
P_COLS = P * TT * (TT + 1) // 2
LOGITS_AT = {0: (4, 0), 1: (4, 2 * P), 2: (5, 0), 3: (6, 0)}
Q_TILES = (3, 2, 1, 0)
PT_AT = {0: 1, 1: 5, 3: 8, 2: 9}
PT_BLOCKS = 11


def yoco_trunk(nc, x_in, c_in, ada_w, ada_b, norm_mix_g, norm_mlp_g, sc_w_in, sc_conv, sc_w_out,
               kv_norm_g, w_kv, k_norm_g, w_f, b_f, q_w, q_norm_g, o_w, mlp_w1, mlp_w2, out):
    top = [-(-nc.sbuf_base // 64) * 64]

    def at(name, shape, dt, offset):
        return nc.alloc_sbuf_tensor_at(name, shape, dt, offset=offset)

    def size(shape, dt):
        n = 2 if dt == BF16 else 4
        for s in shape[1:]:
            n *= s
        return -(-n // 64) * 64

    def new(name, shape, dt):
        offset = top[0]
        top[0] += size(shape, dt)
        return at(name, shape, dt, offset)

    def region(nbytes):
        offset = top[0]
        top[0] += nbytes
        return offset

    def stacked(offset, specs):
        made = []
        for name, shape, dt in specs:
            made.append(at(name, shape, dt, offset))
            offset += size(shape, dt)
        return made

    x = new("x", [P, KT, T], F32)
    act3 = [P, KT, T]
    region_h = region(2 * size(act3, F32))
    h_hi, h_lo = stacked(region_h, [("h_hi", act3, F32R), ("h_lo", act3, F32R)])
    region_g = region(2 * size(act3, F32))
    g_hi, g_lo = stacked(region_g, [("g_hi", act3, F32R), ("g_lo", act3, F32R)])
    ada_first, = stacked(region_g, [("ada_first", [P, KT, 2, D // 2], F32)])
    region_kv = region(4 * size(act3, F32))
    region_o = region_kv + 2 * size(act3, F32)
    (k_hi, k_lo, v_hi, v_lo, pt_hi, pt_lo, probs, qa_hi, qa_lo, qb_hi, qb_lo) = stacked(region_kv, [
        ("k_hi", [P, T], F32R), ("k_lo", [P, T], F32R),
        ("v_hi", [P, TT, P], F32R), ("v_lo", [P, TT, P], F32R),
        ("pt_hi", [P, PT_BLOCKS, P], F32R), ("pt_lo", [P, PT_BLOCKS, P], F32R),
        ("probs", [P, P_COLS], F32),
        ("qa_hi", [P, T], F32R), ("qa_lo", [P, T], F32R),
        ("qb_hi", [P, T], F32R), ("qb_lo", [P, T], F32R)])
    q_pad = [(qa_hi, qa_lo), (qb_hi, qb_lo)]
    o_hi, o_lo = stacked(region_o, [("o_hi", act3, F32R), ("o_lo", act3, F32R)])
    z, ada_acc, ada_raw = stacked(region_kv, [
        ("z", [P, KT, T + CONV - 1], F32), ("ada_acc", [P, NMOD * D], F32),
        ("ada_raw", [P, 2, 2 * D], F32)])
    x_rows, = stacked(region_kv, [("x_rows", [P, TT, D], F32)])
    y_rows, = stacked(region_kv, [("y_rows", [P, KT, TT, P], F32)])
    wf_hi, wf_lo, wf_raw, fg_u, fg_l, fg_a, fg_b, fg_p = stacked(region_o, [
        ("wf_hi", [P, KT, P], F32R), ("wf_lo", [P, KT, P], F32R), ("wf_raw", [P, KT, HEADS], F32),
        ("fg_u", [HEADS, T], F32), ("fg_l", [HEADS, T], F32),
        ("fg_a", [HEADS, T // 2 + T], F32), ("fg_b", [HEADS, T // 2 + T], F32),
        ("fg_p", [HEADS, T], BF16)])
    raw = new("raw", [P, 2, KT, 2 * P], F32)
    w_hi = new("w_hi", [P, 2, KT, P], F32R)
    w_lo = new("w_lo", [P, 2, KT, P], F32R)
    rms = new("rms", [P, T], F32)
    ssum = new("ssum", [P, T], F32)
    ta = new("ta", [P, 2, T], F32)
    tb = new("tb", [P, 2, T], F32)
    tc = new("tc", [P, 2, T], F32)
    ty = new("ty", [P, 2, T], F32)
    tv = new("tv", [P, T], F32)
    ident = new("ident", [P, P], F32)
    ones = new("ones", [P, P], F32)
    ones_head = new("ones_head", [P, P], F32)
    ident_b = new("ident_b", [P, P], BF16)
    mask_b = new("mask_b", [P, P], BF16)
    pick = new("pick", [96, HEADS, P], BF16)
    neg_f = new("neg_f", [96, T], BF16)
    rows_a = new("rows_a", [ROWS, P], F32)
    rows_b = new("rows_b", [2 * NMOD * KT, P], F32)
    cols = new("cols", [P, ROWS], F32)
    ada_bias = new("ada_bias", [P, 2 * NMOD * KT], F32)
    mod = new("mod", [P, 2 * NMOD * KT], F32)
    gains = new("gains", [P, 4, KT], F32)
    c_act = new("c_act", [P, KT], F32)
    c_tmp = new("c_tmp", [P, KT], F32)
    q_gain = new("q_gain", [P, 1], F32)
    eps_col = new("eps_col", [P, 1], F32)
    bf_col = new("bf_col", [HEADS, 1], F32)
    neg_max = new("neg_max", [P, 2 * TT], F32)
    p_sum = new("p_sum", [P, 2 * TT], F32)
    p_inv = new("p_inv", [P, 2 * TT], F32)
    assert top[0] <= nc.sbuf_usable_end, top[0]

    def mcol(layer, part, j):
        k = (layer * NMOD + part) * KT
        return mod[:, k + j:k + j + 1] if isinstance(j, int) else mod[:, bass.ds(j + k, 1)]

    def tile3(t, j):
        return t[:, j, :] if isinstance(j, int) else t[:, bass.ds(j, 1), :].rearrange("p a t -> p (a t)")

    def col(t, j):
        return t[:, j:j + 1] if isinstance(j, int) else t[:, bass.ds(j, 1)]

    with ExitStack() as ctx:
        bank = [ctx.enter_context(nc.psum_tensor(f"bank{i}", [P, T], F32)) for i in range(8)]

        def sem(name):
            return ctx.enter_context(nc.semaphore(name))

        rows_in = sem("rows_in")
        x_loaded = sem("x_loaded")
        wf_loaded = sem("wf_loaded")
        ada_in = [sem(f"ada_in{k}") for k in range(KT)]
        ada_more = [sem("ada_more0"), sem("ada_more1")]
        raw_in = [sem("raw_in0"), sem("raw_in1")]
        half_in = [sem("half_in0"), sem("half_in1")]
        out_done = sem("out_done")
        consts = sem("consts")
        pool_step = sem("pool_step")
        act_step = sem("act_step")
        vec_step = sem("vec_step")
        cols_pe = sem("cols_pe")
        cols_ok = sem("cols_ok")
        silu_e = sem("silu_e")
        c_ok = sem("c_ok")
        ada_used = sem("ada_used")
        ada_pool = sem("ada_pool")
        ada_turned = sem("ada_turned")
        ada_red = sem("ada_red")
        mod_ok = sem("mod_ok")
        x_turned = sem("x_turned")
        x_ok = sem("x_ok")
        sq_ok = sem("sq_ok")
        ss_ok = sem("ss_ok")
        norm_pe = sem("norm_pe")
        norm_y = sem("norm_y")
        norm_v = sem("norm_v")
        norm_ok = sem("norm_ok")
        xn_ok = sem("xn_ok")
        hf_ok = sem("hf_ok")
        hh_ok = sem("hh_ok")
        h_ok = sem("h_ok")
        hi_ok = sem("hi_ok")
        lo_ok = sem("lo_ok")
        pe_done = sem("pe_done")
        bank_free = sem("bank_free")
        conv0 = sem("conv0")
        conv1 = sem("conv1")
        conv2 = sem("conv2")
        pad_ok = sem("pad_ok")
        g_hi_ok = sem("g_hi_ok")
        g_a = sem("g_a")
        g_ok = sem("g_ok")
        hn_sq = sem("hn_sq")
        hn_pe = sem("hn_pe")
        hn_y = sem("hn_y")
        hn_v = sem("hn_v")
        normed = sem("normed")
        v_copied = sem("v_copied")
        k_hi_ok = sem("k_hi_ok")
        k_ok = sem("k_ok")
        v_turned = sem("v_turned")
        v_hi_ok = sem("v_hi_ok")
        v_ok = sem("v_ok")
        wf_hi_ok = sem("wf_hi_ok")
        wf_ok = sem("wf_ok")
        wf_zero = sem("wf_zero")
        fg_pe = sem("fg_pe")
        fg_act = sem("fg_act")
        fg_ok = sem("fg_ok")
        pads_ok = sem("pads_ok")
        qp_hi = sem("qp_hi")
        qp_ok = sem("qp_ok")
        s_ok = sem("s_ok")
        max_ok = sem("max_ok")
        exp_ok = sem("exp_ok")
        p_ok = sem("p_ok")
        t_ok = sem("t_ok")
        pt_hi_ok = sem("pt_hi_ok")
        pt_ok = sem("pt_ok")
        pv_ok = sem("pv_ok")
        o_hi_ok = sem("o_hi_ok")
        o_ok = sem("o_ok")
        y_turned = sem("y_turned")
        y_ok = sem("y_ok")

        block = ctx.enter_context(nc.Block())

        G_CONV, G_MLP0 = 0, KT
        G_MLP1 = KT + CH * KT
        H_MIX0, H_MLP0, H_KV, H_Q, H_MLP1 = 0, 8, 16, 24, 32
        ADA_ORDER = [0, 2, 1, 3] + list(range(4, 2 * NMOD * KT // 4))
        ADA_HALF, ADA_GATE, ADA_MLP, ADA_GATE2, ADA_L1, ADA_ALL = 2, 4, 6, 10, 12, 24
        M_HALF, M_MIX0, M_MLP0, M_MIX1 = 1, 2, 3, 4
        C_IDENT, C_EPS, C_ONES, C_IDENT_B, C_MASK, C_HEAD, C_PICK, C_NEG_F = 1, 2, 3, 4, 5, 7, 8, 9

        @block.sync
        def _(sp):
            def rows(first, src):
                sp.dma_start(rows_a[first:first + src.shape[0], :], src).then_inc(rows_in, 16)

            rows(R_C, c_in.rearrange("a (k p) -> (a k) p", p=P))
            rows(R_MIX, norm_mix_g.rearrange("l (k p) -> (l k) p", p=P))
            rows(R_MLP, norm_mlp_g.rearrange("l (k p) -> (l k) p", p=P))
            rows(R_CONV, sc_conv.rearrange("a w (k p) -> (a w k) p", p=P))
            rows(R_KV, kv_norm_g.rearrange("(k p) -> k p", p=P))
            for half in range(2):
                sp.dma_start(rows_a[R_KN:R_KN + 1, half * HD:(half + 1) * HD],
                             k_norm_g.rearrange("(a n) -> a n", a=1)).then_inc(rows_in, 16)
                sp.dma_start(rows_a[R_QN:R_QN + 1, half * HD:(half + 1) * HD],
                             q_norm_g).then_inc(rows_in, 16)
            sp.dma_start(rows_b[:], ada_b.rearrange("l (k p) -> (l k) p", p=P)).then_inc(rows_in, 16)
            sp.dma_start(bf_col[:], b_f.rearrange("(h a) -> h a", a=1)).then_inc(rows_in, 16)
            sp.dma_start(x_rows[:], x_in[0].rearrange("(t p) d -> p t d", p=P)).then_inc(x_loaded, 16)

            def columns(w, c0=0):
                v = w.rearrange("(k p) n -> p k n", p=P)
                return lambda i: (v[:, :, c0 + i * 2 * P:c0 + (i + 1) * 2 * P] if isinstance(i, int)
                                  else v[:, :, bass.ds(i * (2 * P) + c0, 2 * P)])

            def load_pair(s, source, i):
                sp.dma_start(raw[:, s, :, :], source(i)).then_inc(raw_in[s], 16)

            c_g = columns(sc_w_in[0], D)
            for half in range(2):
                for k in range(KT):
                    if half:
                        sp.wait_ge(ada_used, k + 1)
                    src = ada_w[0, k * P:(k + 1) * P, 0:2 * D].rearrange("p (a b c) -> p a b c", a=2, b=2)
                    sp.dma_start(ada_first[:, k, :, :], src[:, :, half, :]).then_inc(ada_in[k], 16)
                load_pair(half, c_g, half)

            def pairs(first, n, source):
                with sp.Fori(0, n // 2) as i:
                    for s in range(2):
                        sp.wait_ge(lo_ok, 4 * i + 2 * (first + s) - 2)
                        load_pair(s, source, 2 * i + s)

            def mlp(layer, first):
                w1 = mlp_w1[layer].rearrange("(k p) n -> p k n", p=P)
                w2 = mlp_w2[layer].rearrange("(k p) n -> p k n", p=P)
                with sp.Fori(0, CH) as c:
                    pairs(KT * c + first // 2, KT // 2,
                          lambda i: w1[:, :, bass.ds(c * D + i * (2 * P), 2 * P)])
                    pairs(KT * c + (first + KT) // 2, KT // 2,
                          lambda i: w2[:, bass.ds(c * KT, KT), bass.ds(i * (2 * P), 2 * P)])

            for s in range(2):
                sp.wait_ge(lo_ok, 2 * s + 2)
                load_pair(s, c_g, 2 + s)
            pairs(4, 4, columns(sc_w_in[0], 2 * D))
            pairs(8, 4, columns(sc_w_in[0], 0))
            pairs(WOUT // 2, 4, columns(sc_w_out[0]))
            mlp(0, MLP0)
            for (kind, j), b in BLOCK_OF.items():
                half, slot = b % 2, b // 2 % 2
                if half == 0:
                    sp.wait_ge(lo_ok, b - 2)
                src = q_w[0] if kind == "q" else w_kv
                c0 = j * P + (D if kind == "v" else 0)
                sp.dma_start(raw[:, slot, :, half * P:(half + 1) * P],
                             src.rearrange("(k p) n -> p k n", p=P)[:, :, c0:c0 + P]
                             ).then_inc((half_in if half else raw_in)[slot], 16)
            pairs(OUT // 2, 4, columns(o_w[0]))
            mlp(1, MLP1)
            for j in range(KT):
                sp.wait_ge(y_ok, j + 1)
                sp.dma_start(out[0].rearrange("(t p) d -> p t d", p=P)[:, :, j * P:(j + 1) * P],
                             y_rows[:, j, :, :]).then_inc(out_done, 16)
            sp.wait_ge(out_done, 16 * KT)

        @block.gpsimd
        def _(pool):
            steps = [0]

            def link(ins):
                steps[0] += 1
                ins.then_inc(pool_step, 1)
                pool.wait_ge(pool_step, steps[0])

            counted = {}

            def after(ins, signal):
                counted[signal.name] = counted.get(signal.name, 0) + 1
                ins.then_inc(signal, 1)
                pool.wait_ge(signal, counted[signal.name])

            def diagonal(t):
                link(pool.memset(t[:], 0.0))
                after(pool.affine_select(out=t[:], in_=t[:], compare_op=ALU.not_equal, fill=1.0, base=0,
                                         pattern=[[-1, P]], channel_multiplier=1), consts)

            diagonal(ident)
            after(pool.memset(eps_col[:], EPS), consts)
            after(pool.memset(ones[:], 1.0), consts)
            link(pool.memset(ada_acc[:, 2 * D:], 0.0))
            todo = [(0, k, part * D, D) for part in range(2, NMOD) for k in range(KT)]
            todo += [(1, k, part * D, 2 * D) for part in range(0, NMOD, 2) for k in range(KT)]
            last_of_layer_0 = (NMOD - 2) * KT

            def load(i):
                layer, k, c0, n = todo[i]
                if i >= 2:
                    pool.wait_ge(ada_pool, i - 1)
                pool.dma_start(ada_raw[:, i % 2, 0:n],
                               ada_w[layer, k * P:(k + 1) * P, c0:c0 + n]).then_inc(ada_more[i % 2], 16)

            diagonal(ident_b)
            link(pool.memset(mask_b[:], 0.0))
            after(pool.affine_select(out=mask_b[:], in_=mask_b[:], compare_op=ALU.is_ge, fill=MASKED,
                                     base=0, pattern=[[-1, P]], channel_multiplier=1), consts)
            link(pool.memset(ones_head[:], 0.0))
            for half in range(2):
                own = slice(half * HD, (half + 1) * HD)
                after(pool.memset(ones_head[own, own], 1.0), consts)
            link(pool.memset(pick[:], 0.0))
            for part in range(3):
                one = pool.affine_select(out=pick[:], in_=pick[:], compare_op=ALU.not_equal, fill=1.0,
                                         base=-32 * part, pattern=[[-1, HEADS], [0, P]],
                                         channel_multiplier=1)
                if part < 2:
                    link(one)
                else:
                    after(one, consts)
            after(pool.memset(neg_f[:], 0.0), consts)

            pool.wait_ge(c_ok, 1)
            pool.wait_ge(ada_used, KT + KT // 2)
            load(0)
            load(1)
            for i, (layer, k, c0, n) in enumerate(todo):
                if i == last_of_layer_0:
                    pool.wait_ge(ada_turned, ADA_L1)
                    link(pool.memset(ada_acc[:], 0.0))
                if i:
                    pool.wait_ge(ada_pool, i)
                pool.wait_ge(ada_more[i % 2], 16 * (i // 2 + 1))
                acc, part_raw = ada_acc[:, c0:c0 + n], ada_raw[:, i % 2, 0:n]
                link(pool.tensor_tensor(part_raw, part_raw, c_act[:, k:k + 1].to_broadcast([P, n]), ALU.mult))
                pool.tensor_tensor(acc, acc, part_raw, ALU.add).then_inc(ada_pool, 1)
                if i + 2 < len(todo):
                    load(i + 2)

            pool.wait_ge(ada_turned, ADA_ALL)
            pool.dma_start(wf_raw[:], w_f.rearrange("(k p) h -> p k h", p=P)).then_inc(wf_loaded, 16)
            after(pool.memset(wf_hi[:].bitcast(F32), 0.0), wf_zero)
            after(pool.memset(wf_lo[:].bitcast(F32), 0.0), wf_zero)
            link(pool.memset(fg_a[:, 0:T // 2], 0.0))
            link(pool.memset(fg_b[:, 0:T // 2], 0.0))
            for half in range(2):
                other = slice((1 - half) * HD, (2 - half) * HD)
                for t in q_pad[half]:
                    after(pool.memset(t[other, :].bitcast(F32), 0.0), pads_ok)
            after(pool.memset(pt_hi[:, 0, :].bitcast(F32), 0.0), pads_ok)
            after(pool.memset(pt_lo[:, 0, :].bitcast(F32), 0.0), pads_ok)
            half = T // 2
            pool.wait_ge(fg_act, 2)
            link(pool.tensor_scalar(fg_u[:], fg_u[:], 0.0, None, ALU.min))
            link(pool.tensor_tensor(fg_a[:, half:], fg_l[:], fg_u[:], ALU.subtract))
            src, dst, shift = fg_a, fg_b, 1
            while shift < T:
                add = pool.tensor_tensor(dst[:, half:], src[:, half:],
                                         src[:, half - shift:half + T - shift], ALU.add)
                link(add)
                src, dst, shift = dst, src, 2 * shift
            f = src[:, half:]
            link(pool.tensor_copy(neg_f[0:HEADS, :], f))
            link(pool.tensor_tensor(fg_u[:], f, neg_f[0:HEADS, :], ALU.subtract))
            link(pool.tensor_copy(neg_f[32:32 + HEADS, :], fg_u[:]))
            link(pool.tensor_copy(fg_p[:], fg_u[:]))
            pool.tensor_tensor(neg_f[64:64 + HEADS, :], fg_u[:], fg_p[:], ALU.subtract).then_inc(fg_ok, 1)
        @block.tensor
        def _(pe):
            mm, turn = nc.tensor.matmul, nc.tensor.transpose

            def part_of(b, s, out, hi, lo, tiles, ready=None):
                pe.wait_ge(lo_ok, b + 1)
                for k in tiles:
                    if ready:
                        ready(k)
                    mm(out[:], w_hi[:, s, k, :], hi[:, k, :], start=(k == 0), stop=False)
                    mm(out[:], w_hi[:, s, k, :], lo[:, k, :], start=False, stop=False)
                    last = mm(out[:], w_lo[:, s, k, :], hi[:, k, :], start=False, stop=(k == KT - 1))
                return last

            def dense(g, jj, hi, lo, ready=None, between=None):
                if not isinstance(g, int) or g > 0:
                    pe.wait_ge(bank_free, 4 * g + jj - 3)
                b, s, out = 4 * g + jj, jj % 2, bank[jj]
                if between:
                    part_of(b, s, out, hi, lo, range(0, 4), ready)
                    between()
                    last = part_of(b, s, out, hi, lo, range(4, KT), ready)
                else:
                    last = part_of(b, s, out, hi, lo, range(KT), ready)
                last.then_inc(pe_done, 1)

            def layer(first, n, hi, lo, ready):
                with pe.Fori(0, n) as i:
                    for jj in range(GROUP):
                        dense(i + first, jj, hi, lo, ready if jj == 0 else None)

            def norm_sum(n):
                pe.wait_ge(ss_ok, KT * (n + 1))
                mm(bank[4][:], ones[:], ssum[:], start=True, stop=True).then_inc(norm_pe, 1)

            def ada_turn(first, last):
                for n in range(first, last):
                    if n >= 4:
                        pe.wait_ge(ada_red, n - 3)
                    for i in range(4):
                        c = (ADA_ORDER[n] % ADA_L1) * 4 + i
                        t = turn(bank[4 + n % 4][:, i * P:(i + 1) * P], ada_acc[:, c * P:(c + 1) * P], ident[:])
                    t.then_inc(ada_turned, 1)

            pe.wait_ge(consts, C_ONES)
            pe.wait_ge(rows_in, 16 * 11)
            turn(bank[7][:, 0:ROWS], rows_a[:], ident[0:ROWS, 0:ROWS]).then_inc(cols_pe, 1)
            nb = 2 * NMOD * KT
            turn(bank[6][:, 0:nb], rows_b[:], ident[0:nb, 0:nb]).then_inc(cols_pe, 1)
            pe.wait_ge(x_loaded, 16)
            for j in range(KT):
                if j >= 4:
                    pe.wait_ge(x_ok, j - 3)
                for t in range(TT):
                    v = turn(bank[j % 4][:, t * P:(t + 1) * P], x_rows[:, t, j * P:(j + 1) * P], ident[:])
                v.then_inc(x_turned, 1)
            norm_sum(0)
            pe.wait_ge(ada_used, KT)
            pe.wait_ge(norm_v, 1)
            pe.wait_ge(cols_ok, 2)
            ada_turn(0, ADA_HALF)

            pe.wait_ge(x_ok, KT)
            first_h = lambda k: pe.wait_ge(h_ok, H_MIX0 + k + 1)
            for jj in range(2):
                part_of(jj, jj, bank[jj], h_hi, h_lo, range(0, KT // 2), first_h if jj == 0 else None)
            pe.wait_ge(ada_used, 2 * KT)
            ada_turn(ADA_HALF, ADA_GATE)
            for jj in range(2):
                part_of(jj, jj, bank[jj], h_hi, h_lo, range(KT // 2, KT), first_h if jj == 0 else None).then_inc(pe_done, 1)
            for jj in range(2, GROUP):
                dense(0, jj, h_hi, h_lo)
            layer(1, 3 * KT // GROUP - 1, h_hi, h_lo, None)
            pe.wait_ge(ada_pool, KT)
            ada_turn(ADA_GATE, ADA_MLP)
            for jj in range(GROUP):
                dense(WOUT // GROUP, jj, g_hi, g_lo, (lambda k: pe.wait_ge(g_ok, G_CONV + k + 1)) if jj == 0 else None)
            pe.wait_ge(ada_pool, 3 * KT)
            ada_turn(ADA_MLP, ADA_GATE2)
            for jj in range(GROUP):
                dense(WOUT // GROUP + 1, jj, g_hi, g_lo)

            def mlp(first, h_base, g_base, final):
                def chunk(c, between=None):
                    g = first // GROUP + 4 * c
                    layer(g, 2, h_hi, h_lo, lambda k: pe.wait_ge(h_ok, h_base + k + 1))
                    ready = lambda k: pe.wait_ge(g_ok, g_base + KT * c + k + 1)
                    if between is None:
                        layer(g + 2, 2, g_hi, g_lo, ready)
                        return
                    for j in range(KT):
                        dense(g + 2 + j // GROUP, j % GROUP, g_hi, g_lo, ready if j == 0 else None,
                              between(j - 1) if j else None)

                with pe.Fori(0, CH - 1) as c:
                    chunk(c)
                if final:
                    chunk(CH - 1, y_turn)
                    return
                pe.wait_ge(ada_pool, 7 * KT)
                ada_turn(ADA_L1, ADA_L1 + 4)
                g = first // GROUP + 4 * (CH - 1)
                layer(g, 2, h_hi, h_lo, None)
                for i in range(2):
                    ada_turn(ADA_L1 + 4 * (i + 1), ADA_L1 + 4 * (i + 2))
                    for jj in range(GROUP):
                        dense(g + 2 + i, jj, g_hi, g_lo,
                              (lambda k: pe.wait_ge(g_ok, g_base + KT * (CH - 1) + k + 1)) if i + jj == 0 else None)

            def y_turn(j):
                def go():
                    pe.wait_ge(bank_free, BLOCKS - KT + j + 1)
                    if j >= 2:
                        pe.wait_ge(y_ok, j - 1)
                    for t in range(TT):
                        v = turn(bank[4 + j % 2][:, t * P:(t + 1) * P], x[:, j, t * P:(t + 1) * P], ident[:])
                    v.then_inc(y_turned, 1)
                return go

            pe.wait_ge(ada_red, ADA_GATE2)
            norm_sum(1)
            pe.wait_ge(norm_v, 2)
            pe.wait_ge(ada_pool, 4 * KT)
            ada_turn(ADA_GATE2, ADA_L1)
            mlp(MLP0, H_MLP0, G_MLP0, False)
            pe.wait_ge(ada_red, ADA_ALL)
            norm_sum(2)

            EARLY, LATE = range(0, KT // 2), range(KT // 2, KT)

            def kvq(kind, j, tiles, ready=None):
                b = BLOCK_OF[kind, j]
                hi, lo = (g_hi, g_lo) if kind == "q" else (h_hi, h_lo)
                last = part_of(b, b % 2, bank[KVQ_BANK[kind]], hi, lo, tiles, ready)
                if tiles[-1] == KT - 1:
                    last.then_inc(pe_done, 1)

            def head_sum(kind, j):
                pe.wait_ge(hn_sq, NORM_OF[kind, j] + 1)
                mm(bank[MISC][:], ones_head[:], tb[:, 0 if kind == "q" else 1, :], start=True,
                   stop=True).then_inc(hn_pe, 1)

            def v_turn(j):
                pe.wait_ge(v_copied, j + 1)
                for t in range(TT):
                    v = turn(bank[MISC][:, t * P:(t + 1) * P], tb[:, 0, t * P:(t + 1) * P], ident[:])
                v.then_inc(v_turned, 1)

            def logits(h):
                hi, lo = q_pad[h % 2]
                pe.wait_ge(k_ok, h // 2 + 1)
                pe.wait_ge(qp_ok, h + 1)
                if h:
                    pe.wait_ge(pt_ok, 3 * h)
                for qt in Q_TILES:
                    n = max((qt + 1) * P, 2 * P)
                    q_cols = slice(qt * P, (qt + 1) * P)
                    at_bank, c0 = LOGITS_AT[qt]
                    o = bank[at_bank][:, c0:c0 + n]
                    mm(o, hi[:, q_cols], k_hi[:, 0:n], start=True, stop=False)
                    mm(o, hi[:, q_cols], k_lo[:, 0:n], start=False, stop=False)
                    mm(bank[at_bank][:, c0 + qt * P:c0 + (qt + 1) * P], ident_b[:], mask_b[:], start=False,
                       stop=False, skip_group_check=True)
                    mm(o, lo[:, q_cols], k_hi[:, 0:n], start=False, stop=False)
                    mm(o, pick[:, h, :], neg_f[:, 0:n], start=False, stop=True).then_inc(s_ok, 1)

            def turn_probs(h):
                pe.wait_ge(p_ok, h + 1)
                for i, tiles in enumerate(((0,), (1, 3), (2,))):
                    at_col = 0
                    for kt in tiles:
                        for qt in range(kt, TT):
                            v = turn(bank[4 + i][:, at_col:at_col + P],
                                     probs[:, P_OFF[qt] + kt * P:P_OFF[qt] + (kt + 1) * P], ident[:])
                            at_col += P
                    v.then_inc(t_ok, 1)

            def output(h):
                pe.wait_ge(v_ok, h // 2 + 1)
                pe.wait_ge(pt_ok, 3 * (h + 1))
                if h:
                    pe.wait_ge(o_ok, h)

                def prob_t(t, kt):
                    return (t[:, PT_AT[kt]:PT_AT[kt] + TT - kt, :] if kt < 3
                            else t[:, 0:PT_AT[3] + 1:PT_AT[3], :])

                def add(v, kt, t, first=False, end=False):
                    return mm(bank[7][:, min(kt, 2) * P:T], v[:, kt, :], prob_t(t, kt),
                              start=first, stop=end, skip_group_check=True)

                add(v_hi, 0, pt_hi, first=True)
                for kt in range(1, TT):
                    add(v_hi, kt, pt_hi)
                    add(v_hi, kt, pt_lo)
                    add(v_lo, kt, pt_hi)
                add(v_hi, 0, pt_lo)
                last = add(v_lo, 0, pt_hi, end=True)
                last.then_inc(pv_ok, 1)

            pe.wait_ge(consts, C_NEG_F)
            pe.wait_ge(norm_v, 3)
            pe.wait_ge(wf_ok, 1)
            for k in range(KT):
                pe.wait_ge(h_ok, H_KV + k + 1)
                mm(bank[7][:], wf_hi[:, k, :], h_hi[:, k, :], start=(k == 0), stop=False)
                mm(bank[7][:], wf_hi[:, k, :], h_lo[:, k, :], start=False, stop=False)
                f = mm(bank[7][:], wf_lo[:, k, :], h_hi[:, k, :], start=False, stop=(k == KT - 1))
            f.then_inc(fg_pe, 1)
            pe.wait_ge(bank_free, KVQ)
            kvq("k", 0, range(KT))
            kvq("v", 0, EARLY)
            head_sum("k", 0)
            kvq("v", 0, LATE)
            kvq("q", 0, EARLY, lambda k: pe.wait_ge(h_ok, H_Q + k + 1))
            pe.wait_ge(hn_v, 1)
            v_turn(0)
            kvq("q", 0, LATE, lambda k: pe.wait_ge(h_ok, H_Q + k + 1))
            pe.wait_ge(v_ok, 1)
            head_sum("q", 0)
            pe.wait_ge(fg_ok, 1)
            pe.wait_ge(pads_ok, 6)
            for i in range(KT):
                nxt = i + 1
                logits(2 * i)
                if i:
                    output(2 * i - 1)
                    pe.wait_ge(hn_v, NORM_OF["k", i] + 1)
                    v_turn(i)
                if nxt < KT:
                    pe.wait_ge(normed, 2 * nxt)
                    pe.wait_ge(v_copied, nxt)
                    kvq("q", nxt, range(0, 6))
                turn_probs(2 * i)
                if nxt < KT:
                    kvq("q", nxt, range(6, KT))
                    kvq("k", nxt, range(0, 2))
                    pe.wait_ge(v_ok, nxt)
                    pe.wait_ge(hn_v, NORM_OF["q", nxt])
                    head_sum("q", nxt)
                    kvq("k", nxt, range(2, KT))
                logits(2 * i + 1)
                if nxt < KT:
                    pe.wait_ge(hn_v, NORM_OF["k", nxt])
                    head_sum("k", nxt)
                output(2 * i)
                if nxt < KT:
                    kvq("v", nxt, range(0, 3))
                turn_probs(2 * i + 1)
                if nxt < KT:
                    kvq("v", nxt, range(3, KT))
            output(HEADS - 1)
            pe.wait_ge(bank_free, OUT)
            pe.wait_ge(v_ok, KT)
            layer(OUT // GROUP, 2, o_hi, o_lo, lambda k: pe.wait_ge(o_ok, 2 * k + 2))
            norm_sum(3)
            pe.wait_ge(norm_v, 4)
            mlp(MLP1, H_MLP1, G_MLP1, True)
            y_turn(KT - 1)()

        @block.scalar
        def _(act):
            steps = [0]
            go = nc.scalar.activation

            def link(ins):
                steps[0] += 1
                ins.then_inc(act_step, 1)
                act.wait_ge(act_step, steps[0])

            def split(g, jj):
                g, jj = g + jj // GROUP, jj % GROUP
                s, pair = jj % 2, jj // 2
                if isinstance(g, int) and 4 * g + jj in BLOCK_OF.values() and s:
                    act.wait_ge(half_in[pair], 16 * (g - KVQ // 4) + 16)
                else:
                    act.wait_ge(raw_in[pair], 16 * g + 16)
                if not isinstance(g, int) or 4 * g + jj >= 2:
                    act.wait_ge(pe_done, 4 * g + jj - 1)
                go(w_hi[:, s, :, :], raw[:, pair, :, s * P:(s + 1) * P], ACT.Copy).then_inc(hi_ok, 1)

            def groups(first, n, step, written_out=False):
                if written_out:
                    for j in range(n * GROUP):
                        step(first + j // GROUP, j % GROUP, j)
                    return
                with act.Fori(0, n) as i:
                    for jj in range(GROUP):
                        step(i + first, jj, 4 * i + jj)

            def square_tile(m, j, s):
                if not isinstance(m, int) or m >= 2:
                    act.wait_ge(ss_ok, m - 1)
                go(tb[:, s, :], tile3(x, j), ACT.Square).then_inc(sq_ok, 1)

            def norm_root(n):
                act.wait_ge(norm_pe, n + 1)
                link(go(ty[:, 0, :], bank[4][:], ACT.Ln, bias=eps_col[:], scale=1.0 / D))
                go(ty[:, 0, :], ty[:, 0, :], ACT.Exp, scale=-0.5).then_inc(norm_y, 1)
                go(tc[:, 0, :], bank[4][:], ACT.Identity, bias=eps_col[:], scale=1.0 / D).then_inc(norm_v, 1)

            def h_tile(m, j, hi, gain, shift):
                act.wait_ge(xn_ok, m + 1)
                if m >= 2:
                    act.wait_ge(h_ok, m - 1)
                go(ta[:, j % 2, :], tc[:, j % 2, :], ACT.Identity, bias=shift, scale=gain).then_inc(hf_ok, 1)
                act.wait_ge(hf_ok, m + 1)
                go(hi[:, j, :], ta[:, j % 2, :], ACT.Copy).then_inc(hh_ok, 1)

            nc.scalar.preload_act_table_set("natural_log_exp_and_others")
            act.wait_ge(cols_ok, 1)
            go(c_tmp[:], cols[:, R_C:R_C + KT], ACT.Exp, scale=-1.0).then_inc(silu_e, 1)
            for j in range(KT):
                act.wait_ge(x_turned, j + 1)
                go(x[:, j, :], bank[j % 4][:], ACT.Copy).then_inc(x_ok, 1)
                act.wait_ge(x_ok, j + 1)
                square_tile(j, j, j % 2)
            act.wait_ge(consts, C_EPS)
            norm_root(0)
            for jj in range(2):
                split(0, jj)
            for j in range(KT):
                if j % (KT // 2) == 0:
                    act.wait_ge(mod_ok, M_HALF if j == 0 else M_MIX0)
                h_tile(H_MIX0 + j, j, h_hi, gains[:, 0, j:j + 1], mcol(0, 0, j))

            def step_cg(g, jj, j):
                split(g, jj + 2)
                act.wait_ge(pe_done, 4 * g + jj + 1)
                go(z[:, bass.ds(j, 1), CONV - 1:] if not isinstance(j, int) else z[:, j:j + 1, CONV - 1:],
                   bank[jj][:].rearrange("p (a t) -> p a t", a=1), ACT.Copy).then_inc(bank_free, 1)

            def step_xv(g, jj, j):
                split(g, jj + 2)

            def step_bg(g, jj, j):
                act.wait_ge(bank_free, 4 * g + jj - 1)
                z_t = z[:, bass.ds(j, 1), CONV - 1:] if not isinstance(j, int) else z[:, j:j + 1, CONV - 1:]
                go(ta[:, jj % 2, :].rearrange("p (a t) -> p a t", a=1), z_t, ACT.Copy,
                   scale=col(cols, j + (R_CONV + 2 * KT))).then_inc(conv0, 1)
                split(g, jj + 2)
                act.wait_ge(bank_free, 4 * g + jj + 1)
                go(tile3(g_hi, j), tb[:, jj % 2, :], ACT.Copy).then_inc(g_hi_ok, 1)

            groups(WIN // GROUP, 2, step_cg)
            groups(WIN // GROUP + 2, 2, step_xv)
            groups(WIN // GROUP + 4, 2, step_bg)

            def step_proj(base):
                def step(g, jj, j):
                    split(g, jj + 2)
                    act.wait_ge(bank_free, 4 * g + jj + 1)
                    square_tile(j + base, j, jj % 2)
                return step

            act.wait_ge(g_ok, G_CONV + KT)
            groups(WOUT // GROUP, 2, step_proj(KT))
            norm_root(1)
            act.wait_ge(mod_ok, M_MLP0)
            for j in range(KT):
                h_tile(H_MLP0 + j, j, h_hi, gains[:, 1, j:j + 1], mcol(0, 3, j))

            def mlp(first, g_base, ss_base, final):
                def step_up(c):
                    def step(g, jj, j):
                        split(g, jj + 2)
                        act.wait_ge(pe_done, 4 * g + jj + 1)
                        act.wait_ge(bank_free, 4 * g + jj)
                        act.wait_ge(g_ok, KT * c + j + (g_base - 1))
                        go(ta[:, jj % 2, :], bank[jj][:], ACT.Relu).then_inc(bank_free, 1)
                        act.wait_ge(bank_free, 4 * g + jj + 1)
                        go(tile3(g_hi, j), ta[:, jj % 2, :], ACT.Square).then_inc(g_hi_ok, 1)
                    return step

                def step_down(g, jj, j):
                    split(g, jj + 2)

                def step_final(g, jj, j):
                    if j < KT - 2:
                        split(g, jj + 2)
                    if j:
                        y_tile(j - 1)

                def y_tile(j):
                    act.wait_ge(y_turned, j + 1)
                    go(y_rows[:, j, :, :], bank[4 + j % 2][:].rearrange("p (t f) -> p t f", f=P),
                       ACT.Copy).then_inc(y_ok, 1)

                g0 = first // GROUP
                with act.Fori(0, CH - 1) as c:
                    groups(4 * c + g0, 2, step_up(c))
                    groups(4 * c + (g0 + 2), 2, step_down)
                c = CH - 1
                groups(4 * c + g0, 2, step_up(c))
                act.wait_ge(g_ok, g_base + KT * CH)
                if final:
                    groups(4 * c + g0 + 2, 2, step_final, True)
                    y_tile(KT - 1)
                else:
                    groups(4 * c + g0 + 2, 2, step_proj(ss_base), True)

            mlp(MLP0, G_MLP0, 2 * KT, False)
            act.wait_ge(wf_loaded, 16)
            act.wait_ge(wf_zero, 2)
            go(wf_hi[:, :, 0:HEADS], wf_raw[:], ACT.Copy).then_inc(wf_hi_ok, 1)
            norm_root(2)
            for j in range(KT):
                h_tile(H_KV + j, j, h_hi, cols[:, R_KV + j:R_KV + j + 1], 0.0)
            act.wait_ge(fg_pe, 1)
            go(fg_u[:], bank[7][0:HEADS, :], ACT.Identity, bias=bf_col[:]).then_inc(fg_act, 1)
            link(go(fg_l[:], bank[7][0:HEADS, :], ACT.Abs, bias=bf_col[:]))
            link(go(fg_l[:], fg_l[:], ACT.Exp, scale=-1.0))
            go(fg_l[:], fg_l[:], ACT.Ln, bias=ones[0:HEADS, 0:1]).then_inc(fg_act, 1)

            def after_block(kind, j):
                b = BLOCK_OF[kind, j] + 2
                split(b // GROUP, b % GROUP)

            def head_square(kind, j):
                act.wait_ge(pe_done, BLOCK_OF[kind, j] + 1)
                if kind == "q":
                    act.wait_ge(v_turned, max(j, 1))
                elif j:
                    act.wait_ge(hn_pe, NORM_OF["k", j - 1] + 1)
                go(tb[:, 0 if kind == "q" else 1, :], bank[KVQ_BANK[kind]][:], ACT.Square).then_inc(hn_sq, 1)

            def head_root(kind, j):
                act.wait_ge(hn_pe, NORM_OF[kind, j] + 1)
                if kind == "q":
                    if j:
                        act.wait_ge(qp_ok, 2 * j)
                elif j:
                    act.wait_ge(k_ok, j)
                v, y = (tc[:, 0, :], ty[:, 0, :]) if kind == "q" else (tv[:], ty[:, 1, :])
                link(go(y, bank[MISC][:], ACT.Ln, bias=eps_col[:], scale=1.0 / HD))
                go(y, y, ACT.Exp, scale=-0.5).then_inc(hn_y, 1)
                go(v, bank[MISC][:], ACT.Identity, bias=eps_col[:], scale=1.0 / HD).then_inc(hn_v, 1)

            def k_high(j):
                act.wait_ge(normed, NORM_OF["k", j] + 1)
                if j:
                    act.wait_ge(s_ok, 2 * TT * j)
                go(k_hi[:], ty[:, 1, :], ACT.Copy).then_inc(k_hi_ok, 1)

            def v_copy(j):
                act.wait_ge(pe_done, BLOCK_OF["v", j] + 1)
                if j:
                    act.wait_ge(hn_pe, NORM_OF["q", j] + 1)
                go(tb[:, 0, :], bank[KVQ_BANK["v"]][:], ACT.Copy).then_inc(v_copied, 1)

            def v_high(j):
                act.wait_ge(v_turned, j + 1)
                if j:
                    act.wait_ge(pv_ok, 2 * j)
                go(v_hi[:], bank[MISC][:].rearrange("p (t f) -> p t f", f=P), ACT.Copy).then_inc(v_hi_ok, 1)

            def q_high(h):
                half = h % 2
                own = slice(half * HD, (half + 1) * HD)
                act.wait_ge(normed, NORM_OF["q", h // 2] + 1)
                if h >= 2:
                    act.wait_ge(s_ok, TT * (h - 1))
                go(q_pad[half][0][own, :], ty[own, 0, :], ACT.Copy).then_inc(qp_hi, 1)

            def exponentials(h):
                for i, qt in enumerate(Q_TILES):
                    s = TT * (h % 2) + i
                    n = (qt + 1) * P
                    at_bank, c0 = LOGITS_AT[qt]
                    act.wait_ge(max_ok, TT * h + (i + 1 if i < 2 else TT))
                    if i == 0 and h:
                        act.wait_ge(t_ok, 3 * h)
                        act.wait_ge(p_ok, h)
                    go(probs[:, P_OFF[qt]:P_OFF[qt] + n], bank[at_bank][:, c0:c0 + n], ACT.Exp,
                       bias=neg_max[:, s:s + 1], accum_out=p_sum[:, s:s + 1]).then_inc(exp_ok, 1)

            def probs_high(h):
                for i in range(3):
                    act.wait_ge(t_ok, 3 * h + i + 1)
                    if h:
                        act.wait_ge(pv_ok, h)
                    first, n = ((1, 4), (5, 4), (9, 2))[i]
                    go(pt_hi[:, first:first + n, :],
                       bank[4 + i][:, 0:n * P].rearrange("p (b c) -> p b c", c=P),
                       ACT.Copy).then_inc(pt_hi_ok, 1)

            def out_high(h):
                own = slice((h % 2) * HD, (h % 2 + 1) * HD)
                act.wait_ge(pv_ok, h + 1)
                go(o_hi[own, h // 2, :], bank[7][own, :], ACT.Copy).then_inc(o_hi_ok, 1)

            act.wait_ge(ss_ok, 3 * KT)
            act.wait_ge(mod_ok, M_MIX1)

            def query_input(first, last):
                for j in range(first, last):
                    h_tile(H_Q + j, j, g_hi, gains[:, 2, j:j + 1], mcol(1, 0, j))

            query_input(0, KT // 2)
            head_square("k", 0)
            after_block("k", 0)
            query_input(KT // 2, KT)
            head_root("k", 0)
            v_copy(0)
            after_block("v", 0)
            k_high(0)
            v_high(0)
            head_square("q", 0)
            after_block("q", 0)
            head_root("q", 0)
            q_high(0)
            q_high(1)
            for i in range(KT):
                nxt = i + 1
                exponentials(2 * i)
                if i:
                    out_high(2 * i - 1)
                    v_high(i)
                    after_block("v", i)
                probs_high(2 * i)
                if nxt < KT:
                    head_square("q", nxt)
                    after_block("q", nxt)
                    head_root("q", nxt)
                    head_square("k", nxt)
                exponentials(2 * i + 1)
                if nxt < KT:
                    head_root("k", nxt)
                out_high(2 * i)
                if nxt < KT:
                    q_high(2 * nxt)
                probs_high(2 * i + 1)
                if nxt < KT:
                    k_high(nxt)
                    after_block("k", nxt)
                    q_high(2 * nxt + 1)
                    v_copy(nxt)
            out_high(HEADS - 1)

            groups(OUT // GROUP, 2, step_proj(3 * KT))
            norm_root(3)
            for j in range(KT):
                h_tile(H_MLP1 + j, j, h_hi, gains[:, 3, j:j + 1], mcol(1, 3, j))
            mlp(MLP1, G_MLP1, 4 * KT, True)

        @block.vector
        def _(dve):
            steps = [0]
            tt, stt, ts = nc.vector.tensor_tensor, nc.vector.scalar_tensor_tensor, nc.vector.tensor_scalar

            def link(ins):
                steps[0] += 1
                ins.then_inc(vec_step, 1)
                dve.wait_ge(vec_step, steps[0])

            def split(g, jj):
                g, jj = g + jj // GROUP, jj % GROUP
                s, pair = jj % 2, jj // 2
                dve.wait_ge(hi_ok, 4 * g + jj + 1)
                tt(w_lo[:, s, :, :], raw[:, pair, :, s * P:(s + 1) * P], w_hi[:, s, :, :],
                   ALU.subtract).then_inc(lo_ok, 1)

            def groups(first, n, step, written_out=False, j0=0):
                if written_out:
                    for j in range(n * GROUP):
                        step(first + j // GROUP, j % GROUP, j0 + j)
                    return
                with dve.Fori(0, n) as i:
                    for jj in range(GROUP):
                        step(i + first, jj, 4 * i + jj)

            def add_square(m, s):
                dve.wait_ge(sq_ok, m + 1)
                if not isinstance(m, int) or m:
                    dve.wait_ge(ss_ok, m)
                tt(ssum[:], ssum[:], tb[:, s, :], ALU.add).then_inc(ss_ok, 1)

            def refine_start(dst, y):
                link(stt(out=dst, in0=y, scalar=-0.5, in1=y, op0=ALU.mult, op1=ALU.mult))

            def refine_end(dst, v, y):
                link(tt(dst, dst, v, ALU.mult))
                link(stt(out=dst, in0=dst, scalar=1.5, in1=y, op0=ALU.add, op1=ALU.mult))

            def norm_end(n):
                dve.wait_ge(norm_y, n + 1)
                refine_start(rms[:], ty[:, 0, :])
                dve.wait_ge(norm_v, n + 1)
                refine_end(rms[:], tc[:, 0, :], ty[:, 0, :])

            def xn(m, j):
                if m >= 2:
                    dve.wait_ge(hh_ok, m - 1)
                tt(tc[:, j % 2, :], x[:, j, :], rms[:], ALU.mult).then_inc(xn_ok, 1)

            def h_low(m, j, hi, lo):
                dve.wait_ge(hh_ok, m + 1)
                tt(lo[:, j, :], ta[:, j % 2, :], hi[:, j, :], ALU.subtract).then_inc(h_ok, 1)

            def make_h(base, hi, lo, first=0, last=KT):
                xn(base + first, first)
                xn(base + first + 1, first + 1)
                for j in range(first, last):
                    h_low(base + j, j, hi, lo)
                    if j + 2 < last:
                        xn(base + j + 2, j + 2)

            def ada_reduce(first, last):
                for n in range(first, last):
                    g = ADA_ORDER[n]
                    dve.wait_ge(ada_turned, n + 1)
                    nc.vector.tensor_reduce(mod[:, 4 * g:4 * g + 4], bank[4 + n % 4][:].rearrange("p (a b) -> p a b", b=P),
                                            AX_X, ALU.add).then_inc(ada_red, 1)
                dve.wait_ge(ada_red, last)
                for n in range(first, last):
                    part = slice(4 * ADA_ORDER[n], 4 * ADA_ORDER[n] + 4)
                    done = tt(mod[:, part], mod[:, part], ada_bias[:, part], ALU.add)
                link(done)

            def gain(n, layer, part, row, tiles=(0, KT)):
                k = (layer * NMOD + part) * KT
                return stt(out=gains[:, n, tiles[0]:tiles[1]], in0=mod[:, k + tiles[0]:k + tiles[1]], scalar=1.0,
                           in1=cols[:, row + tiles[0]:row + tiles[1]], op0=ALU.add, op1=ALU.mult)

            def ada_first_step(half, k):
                n = half * KT + k
                dve.wait_ge(ada_in[k], 16 * (half + 1))
                acc = ada_acc[:, 0:2 * D].rearrange("p (a b c) -> p a b c", a=2, b=2)[:, :, half, :]
                if k == 0:
                    one = ts(acc, ada_first[:, k, :, :], c_act[:, 0:1], None, ALU.mult)
                else:
                    dve.wait_ge(ada_used, n)
                    one = stt(out=acc, in0=ada_first[:, k, :, :], scalar=c_act[:, k:k + 1], in1=acc,
                              op0=ALU.mult, op1=ALU.add)
                one.then_inc(ada_used, 1)

            dve.wait_ge(cols_pe, 1)
            nc.vector.tensor_copy(cols[:], bank[7][:, 0:ROWS]).then_inc(cols_ok, 1)
            dve.wait_ge(cols_pe, 2)
            nc.vector.tensor_copy(ada_bias[:], bank[6][:, 0:2 * NMOD * KT]).then_inc(cols_ok, 1)
            dve.wait_ge(silu_e, 1)
            dve.wait_ge(cols_ok, 2)
            link(ts(c_tmp[:], c_tmp[:], 1.0, None, ALU.add))
            link(nc.vector.reciprocal(c_tmp[:], c_tmp[:]))
            tt(c_act[:], cols[:, R_C:R_C + KT], c_tmp[:], ALU.mult).then_inc(c_ok, 1)
            link(ts(q_gain[:], cols[:, R_QN:R_QN + 1], HD ** -0.5, None, ALU.mult))
            link(nc.vector.memset(ssum[:], 0.0))
            dve.wait_ge(c_ok, 1)
            for j in range(KT):
                add_square(j, j % 2)
                ada_first_step(0, j)
            norm_end(0)
            dve.wait_ge(x_turned, KT)
            link(nc.vector.memset(z[:, :, 0:CONV - 1], 0.0))
            ada_reduce(0, ADA_HALF)
            gain(0, 0, 1, R_MIX, (0, KT // 2)).then_inc(mod_ok, 1)
            split(0, 0)
            make_h(H_MIX0, h_hi, h_lo, 0, KT // 2)
            split(0, 1)
            for k in range(KT):
                ada_first_step(1, k)
            ada_reduce(ADA_HALF, ADA_GATE)
            gain(0, 0, 1, R_MIX, (KT // 2, KT)).then_inc(mod_ok, 1)
            make_h(H_MIX0, h_hi, h_lo, KT // 2, KT)

            def step_cg(g, jj, j):
                split(g, jj + 2)

            def step_xv(g, jj, j):
                split(g, jj + 2)
                dve.wait_ge(pe_done, 4 * g + jj + 1)
                dve.wait_ge(bank_free, 4 * g + jj)
                z_t = z[:, bass.ds(j, 1), CONV - 1:]
                tt(z_t, bank[jj][:].rearrange("p (a t) -> p a t", a=1), z_t, ALU.mult).then_inc(bank_free, 1)

            def step_bg(g, jj, j):
                s = jj % 2
                acc = ta[:, s, :].rearrange("p (a t) -> p a t", a=1)
                dve.wait_ge(conv0, j + 1)
                stt(out=acc, in0=z[:, bass.ds(j, 1), 1:T + 1], scalar=col(cols, j + (R_CONV + KT)), in1=acc,
                    op0=ALU.mult, op1=ALU.add).then_inc(conv1, 1)
                dve.wait_ge(conv1, j + 1)
                stt(out=acc, in0=z[:, bass.ds(j, 1), 0:T], scalar=col(cols, j + R_CONV), in1=acc,
                    op0=ALU.mult, op1=ALU.add).then_inc(conv2, 1)
                split(g, jj + 2)
                dve.wait_ge(pe_done, 4 * g + jj + 1)
                dve.wait_ge(conv2, j + 1)
                tt(tb[:, s, :], bank[jj][:], ta[:, s, :], ALU.mult).then_inc(bank_free, 1)
                dve.wait_ge(g_hi_ok, j + 1)
                dve.wait_ge(bank_free, 4 * g + jj + 1)
                tt(tile3(g_lo, j), tb[:, s, :], tile3(g_hi, j), ALU.subtract).then_inc(g_ok, 1)

            groups(WIN // GROUP, 2, step_cg)
            groups(WIN // GROUP + 2, 2, step_xv)
            groups(WIN // GROUP + 4, 2, step_bg)

            def step_proj(layer, part, base):
                def step(g, jj, j):
                    split(g, jj + 2)
                    dve.wait_ge(pe_done, 4 * g + jj + 1)
                    dve.wait_ge(bank_free, 4 * g + jj)
                    stt(out=tile3(x, j), in0=bank[jj][:], scalar=mcol(layer, part, j), in1=tile3(x, j),
                        op0=ALU.mult, op1=ALU.add).then_inc(bank_free, 1)
                    if base:
                        add_square(j + base, jj % 2)
                return step

            ada_reduce(ADA_GATE, ADA_MLP)
            link(nc.vector.memset(ssum[:], 0.0))
            groups(WOUT // GROUP, 1, step_proj(0, 2, KT), True)
            ada_reduce(ADA_MLP, ADA_GATE2)
            gain(1, 0, 4, R_MLP).then_inc(mod_ok, 1)
            groups(WOUT // GROUP + 1, 1, step_proj(0, 2, KT), True, GROUP)
            norm_end(1)
            make_h(H_MLP0, h_hi, h_lo)
            ada_reduce(ADA_GATE2, ADA_L1)

            def mlp(layer, first, g_base, ss_base, final):
                def step_up(c):
                    def step(g, jj, j):
                        s = jj % 2
                        split(g, jj + 2)
                        dve.wait_ge(bank_free, 4 * g + jj + 1)
                        tt(tb[:, s, :], ta[:, s, :], ta[:, s, :], ALU.mult).then_inc(g_a, 1)
                        dve.wait_ge(g_a, KT * c + j + (g_base - KT + 1))
                        dve.wait_ge(g_hi_ok, KT * c + j + (g_base + 1))
                        tt(tile3(g_lo, j), tb[:, s, :], tile3(g_hi, j), ALU.subtract).then_inc(g_ok, 1)
                    return step

                def step_final(g, jj, j):
                    if j < KT - 2:
                        split(g, jj + 2)
                    dve.wait_ge(pe_done, 4 * g + jj + 1)
                    dve.wait_ge(bank_free, 4 * g + jj)
                    stt(out=x[:, j, :], in0=bank[jj][:], scalar=mcol(layer, 5, j), in1=x[:, j, :],
                        op0=ALU.mult, op1=ALU.add).then_inc(bank_free, 1)

                g0 = first // GROUP
                with dve.Fori(0, CH - 1) as c:
                    groups(4 * c + g0, 2, step_up(c))
                    groups(4 * c + (g0 + 2), 2, step_proj(layer, 5, None))
                c = CH - 1
                if final:
                    groups(4 * c + g0, 2, step_up(c))
                    groups(4 * c + g0 + 2, 2, step_final, True)
                    return
                ada_reduce(ADA_L1, ADA_L1 + 4)
                gain(2, 1, 1, R_MIX + KT).then_inc(mod_ok, 1)
                link(nc.vector.memset(ssum[:], 0.0))
                groups(4 * c + g0, 2, step_up(c))
                for i in range(2):
                    ada_reduce(ADA_L1 + 4 * (i + 1), ADA_L1 + 4 * (i + 2))
                    groups(4 * c + g0 + 2 + i, 1, step_proj(layer, 5, ss_base), True, GROUP * i)
                link(gain(3, 1, 4, R_MLP + KT))

            mlp(0, MLP0, G_MLP0, 2 * KT, False)
            dve.wait_ge(wf_hi_ok, 1)
            tt(wf_lo[:, :, 0:HEADS], wf_raw[:], wf_hi[:, :, 0:HEADS], ALU.subtract).then_inc(wf_ok, 1)
            norm_end(2)
            make_h(H_KV, h_hi, h_lo)

            def after_block(kind, j):
                b = BLOCK_OF[kind, j] + 2
                split(b // GROUP, b % GROUP)

            def root_of(kind):
                return (tc[:, 0, :], ty[:, 0, :]) if kind == "q" else (tv[:], ty[:, 1, :])

            def head_norm(kind, j):
                v, y = root_of(kind)
                n = NORM_OF[kind, j]
                dve.wait_ge(hn_y, n + 1)
                if n:
                    dve.wait_ge(normed, n)
                refine_start(ssum[:], y)
                dve.wait_ge(hn_v, n + 1)
                refine_end(ssum[:], v, y)
                stt(out=y, in0=bank[KVQ_BANK[kind]][:], scalar=q_gain[:] if kind == "q" else cols[:, R_KN:R_KN + 1],
                    in1=ssum[:], op0=ALU.mult, op1=ALU.mult).then_inc(normed, 1)

            def k_low(j):
                dve.wait_ge(k_hi_ok, j + 1)
                tt(k_lo[:], ty[:, 1, :], k_hi[:], ALU.subtract).then_inc(k_ok, 1)

            def v_low(j):
                dve.wait_ge(v_hi_ok, j + 1)
                tt(v_lo[:], bank[MISC][:].rearrange("p (t f) -> p t f", f=P), v_hi[:],
                   ALU.subtract).then_inc(v_ok, 1)

            def q_low(h):
                own = slice((h % 2) * HD, (h % 2 + 1) * HD)
                hi, lo = q_pad[h % 2]
                dve.wait_ge(qp_hi, h + 1)
                tt(lo[own, :], ty[own, 0, :], hi[own, :], ALU.subtract).then_inc(qp_ok, 1)

            def softmax(h):
                slots = slice(TT * (h % 2), TT * (h % 2) + TT)
                for i, qt in enumerate(Q_TILES):
                    s = TT * (h % 2) + i
                    at_bank, c0 = LOGITS_AT[qt]
                    dve.wait_ge(s_ok, TT * h + (i + 1 if i < 2 else TT))
                    if h >= 2 and i == 0:
                        dve.wait_ge(exp_ok, TT * (h - 1))
                    nc.vector.tensor_reduce(neg_max[:, s:s + 1], bank[at_bank][:, c0:c0 + (qt + 1) * P], AX_X,
                                            ALU.max, negate=True).then_inc(max_ok, 1)
                dve.wait_ge(exp_ok, TT * (h + 1))
                link(nc.vector.reciprocal(p_inv[:, slots], p_sum[:, slots]))
                for i, qt in enumerate(Q_TILES):
                    p = probs[:, P_OFF[qt]:P_OFF[qt] + (qt + 1) * P]
                    s = TT * (h % 2) + i
                    one = ts(p, p, p_inv[:, s:s + 1], None, ALU.mult)
                one.then_inc(p_ok, 1)

            def probs_low(h):
                for i in range(3):
                    dve.wait_ge(pt_hi_ok, 3 * h + i + 1)
                    first, n = ((1, 4), (5, 4), (9, 2))[i]
                    tt(pt_lo[:, first:first + n, :],
                       bank[4 + i][:, 0:n * P].rearrange("p (b c) -> p b c", c=P),
                       pt_hi[:, first:first + n, :], ALU.subtract).then_inc(pt_ok, 1)

            def out_low(h):
                own = slice((h % 2) * HD, (h % 2 + 1) * HD)
                dve.wait_ge(o_hi_ok, h + 1)
                tt(o_lo[own, h // 2, :], bank[7][own, :], o_hi[own, h // 2, :], ALU.subtract).then_inc(o_ok, 1)

            make_h(H_Q, g_hi, g_lo, 0, KT // 2)
            after_block("k", 0)
            make_h(H_Q, g_hi, g_lo, KT // 2, KT)
            after_block("v", 0)
            head_norm("k", 0)
            k_low(0)
            v_low(0)
            after_block("q", 0)
            head_norm("q", 0)
            q_low(0)
            q_low(1)
            for i in range(KT):
                nxt = i + 1
                softmax(2 * i)
                if i:
                    out_low(2 * i - 1)
                    v_low(i)
                    after_block("v", i)
                probs_low(2 * i)
                if nxt < KT:
                    after_block("q", nxt)
                    head_norm("q", nxt)
                softmax(2 * i + 1)
                if nxt < KT:
                    head_norm("k", nxt)
                    q_low(2 * nxt)
                probs_low(2 * i + 1)
                if nxt < KT:
                    k_low(nxt)
                out_low(2 * i)
                if nxt < KT:
                    after_block("k", nxt)
                    q_low(2 * nxt + 1)
            out_low(HEADS - 1)

            dve.wait_ge(normed, 2 * KT)
            dve.wait_ge(v_copied, KT)
            nc.vector.memset(ssum[:], 0.0).then_inc(bank_free, OUT - KVQ)
            dve.wait_ge(bank_free, OUT)
            groups(OUT // GROUP, 2, step_proj(1, 2, 3 * KT))
            norm_end(3)
            make_h(H_MLP1, h_hi, h_lo)
            mlp(1, MLP1, G_MLP1, 4 * KT, True)


_INS = ["x", "c", "ada_w", "ada_b", "norm_mix_g", "norm_mlp_g", "sc_w_in", "sc_conv", "sc_w_out",
        "kv_norm_g", "w_kv", "k_norm_g", "w_f", "b_f", "q_w", "q_norm_g", "o_w", "mlp_w1", "mlp_w2"]


def kernel(**inputs):
    import numpy as np
    import concourse.bacc as bacc
    from concourse.bass_utils import run_bass_kernel_spmd

    nc = bacc.Bacc("TRN2", target_bir_lowering=False, num_devices=1)
    arrays, args = {}, []
    for name in _INS:
        a = np.ascontiguousarray(inputs[name])
        arrays[f"in_{name}"] = a
        args.append(nc.dram_tensor(f"in_{name}", a.shape, mybir.dt.from_np(a.dtype), kind="ExternalInput").ap())
    out = nc.dram_tensor("out", arrays["in_x"].shape, F32, kind="ExternalOutput").ap()
    yoco_trunk(nc, *args, out)
    r = run_bass_kernel_spmd(nc, [arrays], core_ids=[0])
    return r.results[0]["out"]
```

```python
from contextlib import ExitStack

import concourse.bass as bass
from concourse import mybir

F32 = mybir.dt.float32
F32R = mybir.dt.float32r
BF16 = mybir.dt.bfloat16
ALU = mybir.AluOpType
ACT = mybir.ActivationFunctionType
AX_X = mybir.AxisListType.X

P = 128
D = 1024
T = 512
KT = D // P
TT = T // P
FF = 4 * D
CH = FF // D
HEADS = 16
HD = D // HEADS
CONV = 3
NMOD = 6
EPS = 1e-6
MASKED = -1e30

WIN = 0
WOUT = WIN + 3 * KT
MLP0 = WOUT + KT
KVQ = MLP0 + 2 * CH * KT
OUT = KVQ + 3 * KT
MLP1 = OUT + KT
BLOCKS = MLP1 + 2 * CH * KT
GROUP = 4

KVQ_ORDER = [("k", 0), ("v", 0), ("k", 1), ("q", 0), ("q", 1), ("v", 1)]
KVQ_ORDER += [(kind, j) for j in range(2, KT) for kind in "qkv"]
BLOCK_OF = {name: KVQ + n for n, name in enumerate(KVQ_ORDER)}
NORM_ORDER = [("k", 0), ("q", 0), ("k", 1), ("q", 1)] + [(kind, j) for j in range(2, KT) for kind in "qk"]
NORM_OF = {name: n for n, name in enumerate(NORM_ORDER)}
SQUARE_OF = {name: n for n, name in enumerate(name for name in KVQ_ORDER if name[0] != "v")}
KVQ_BANK = {(kind, j): "qkv".index(kind) for kind, j in KVQ_ORDER}
KVQ_BANK["k", 1] = 7
MISC = 3
SUM_BANK = {name: MISC for name in KVQ_ORDER}
SUM_BANK["q", 0] = 5

R_C, R_MIX, R_MLP, R_CONV, R_KV, R_KN, R_QN = 0, 8, 24, 40, 64, 72, 73
ROWS = 74

P_OFF = [P * (qt * (qt + 1) // 2) for qt in range(TT)]
P_COLS = P * TT * (TT + 1) // 2
LOGITS_AT = {0: (4, 0), 1: (4, 2 * P), 2: (5, 0), 3: (6, 0)}
Q_TILES = (3, 2, 1, 0)
PT_AT = {0: 1, 1: 5, 3: 8, 2: 9}
PT_BLOCKS = 11


def yoco_trunk(nc, x_in, c_in, ada_w, ada_b, norm_mix_g, norm_mlp_g, sc_w_in, sc_conv, sc_w_out,
               kv_norm_g, w_kv, k_norm_g, w_f, b_f, q_w, q_norm_g, o_w, mlp_w1, mlp_w2, out):
    top = [-(-nc.sbuf_base // 64) * 64]

    def at(name, shape, dt, offset):
        return nc.alloc_sbuf_tensor_at(name, shape, dt, offset=offset)

    def size(shape, dt):
        n = 2 if dt == BF16 else 4
        for s in shape[1:]:
            n *= s
        return -(-n // 64) * 64

    def new(name, shape, dt):
        offset = top[0]
        top[0] += size(shape, dt)
        return at(name, shape, dt, offset)

    def region(nbytes):
        offset = top[0]
        top[0] += nbytes
        return offset

    def stacked(offset, specs):
        made = []
        for name, shape, dt in specs:
            made.append(at(name, shape, dt, offset))
            offset += size(shape, dt)
        return made

    x = new("x", [P, KT, T], F32)
    act3 = [P, KT, T]
    region_h = region(2 * size(act3, F32))
    h_hi, h_lo = stacked(region_h, [("h_hi", act3, F32R), ("h_lo", act3, F32R)])
    region_g = region(2 * size(act3, F32))
    g_hi, g_lo = stacked(region_g, [("g_hi", act3, F32R), ("g_lo", act3, F32R)])
    ada_first, = stacked(region_g, [("ada_first", [P, KT, 2, D // 2], F32)])
    region_kv = region(4 * size(act3, F32))
    region_o = region_kv + 2 * size(act3, F32)
    (k_hi, k_lo, v_hi, v_lo, pt_hi, pt_lo, probs, qa_hi, qa_lo, qb_hi, qb_lo) = stacked(region_kv, [
        ("k_hi", [P, T], F32R), ("k_lo", [P, T], F32R),
        ("v_hi", [P, TT, P], F32R), ("v_lo", [P, TT, P], F32R),
        ("pt_hi", [P, PT_BLOCKS, P], F32R), ("pt_lo", [P, PT_BLOCKS, P], F32R),
        ("probs", [P, P_COLS], F32),
        ("qa_hi", [P, T], F32R), ("qa_lo", [P, T], F32R),
        ("qb_hi", [P, T], F32R), ("qb_lo", [P, T], F32R)])
    q_pad = [(qa_hi, qa_lo), (qb_hi, qb_lo)]
    o_hi, o_lo = stacked(region_o, [("o_hi", act3, F32R), ("o_lo", act3, F32R)])
    z, ada_acc, ada_raw = stacked(region_kv, [
        ("z", [P, KT, T + CONV - 1], F32), ("ada_acc", [P, NMOD * D], F32),
        ("ada_raw", [P, 2, 2 * D], F32)])
    x_rows, = stacked(region_kv, [("x_rows", [P, TT, D], F32)])
    y_rows, = stacked(region_kv, [("y_rows", [P, KT, TT, P], F32)])
    wf_hi, wf_lo, wf_raw, fg_u, fg_l, fg_f, fg_p = stacked(region_o, [
        ("wf_hi", [P, KT, P], F32R), ("wf_lo", [P, KT, P], F32R), ("wf_raw", [P, KT, HEADS], F32),
        ("fg_u", [HEADS, T], F32), ("fg_l", [HEADS, T], F32),
        ("fg_f", [HEADS, T], F32),
        ("fg_p", [HEADS, T], BF16)])
    raw = new("raw", [P, 2, KT, 2 * P], F32)
    w_hi = new("w_hi", [P, 2, KT, P], F32R)
    w_lo = new("w_lo", [P, 2, KT, P], F32R)
    rms = new("rms", [P, T], F32)
    ssum = new("ssum", [P, T], F32)
    ta = new("ta", [P, 2, T], F32)
    tb = new("tb", [P, 2, T], F32)
    tc = new("tc", [P, 2, T], F32)
    ty = new("ty", [P, 2, T], F32)
    tv = new("tv", [P, T], F32)
    ident = new("ident", [P, P], F32)
    ones = new("ones", [P, P], F32)
    ones_head = new("ones_head", [P, P], F32)
    ident_b = new("ident_b", [P, P], BF16)
    mask_b = new("mask_b", [P, P], BF16)
    pick = new("pick", [96, HEADS, P], BF16)
    neg_f = new("neg_f", [96, T], BF16)
    rows_a = new("rows_a", [ROWS, P], F32)
    rows_b = new("rows_b", [2 * NMOD * KT, P], F32)
    cols = new("cols", [P, ROWS], F32)
    ada_bias = new("ada_bias", [P, 2 * NMOD * KT], F32)
    mod = new("mod", [P, 2 * NMOD * KT], F32)
    gains = new("gains", [P, 4, KT], F32)
    c_act = new("c_act", [P, KT], F32)
    c_tmp = new("c_tmp", [P, KT], F32)
    q_gain = new("q_gain", [P, 1], F32)
    eps_col = new("eps_col", [P, 1], F32)
    bf_col = new("bf_col", [HEADS, 1], F32)
    neg_max = new("neg_max", [P, 2 * TT], F32)
    p_sum = new("p_sum", [P, 2 * TT], F32)
    p_inv = new("p_inv", [P, 2 * TT], F32)
    assert top[0] <= nc.sbuf_usable_end, top[0]

    def mcol(layer, part, j):
        k = (layer * NMOD + part) * KT
        return mod[:, k + j:k + j + 1] if isinstance(j, int) else mod[:, bass.ds(j + k, 1)]

    def hs_slot(j, cols):
        return (tc, ta)[j // 2 % 2][:, j % 2, cols]

    def tile3(t, j):
        return t[:, j, :] if isinstance(j, int) else t[:, bass.ds(j, 1), :].rearrange("p a t -> p (a t)")

    def col(t, j):
        return t[:, j:j + 1] if isinstance(j, int) else t[:, bass.ds(j, 1)]

    with ExitStack() as ctx:
        bank = [ctx.enter_context(nc.psum_tensor(f"bank{i}", [P, T], F32)) for i in range(8)]

        def sem(name):
            return ctx.enter_context(nc.semaphore(name))

        rows_in = sem("rows_in")
        x_loaded = sem("x_loaded")
        wf_loaded = sem("wf_loaded")
        ada_in = [sem(f"ada_in{k}") for k in range(KT)]
        ada_more = [sem("ada_more0"), sem("ada_more1")]
        raw_in = [sem("raw_in0"), sem("raw_in1")]
        half_in = [sem("half_in0"), sem("half_in1")]
        out_done = sem("out_done")
        consts = sem("consts")
        pool_step = sem("pool_step")
        act_step = sem("act_step")
        vec_step = sem("vec_step")
        cols_pe = sem("cols_pe")
        cols_ok = sem("cols_ok")
        silu_e = sem("silu_e")
        c_ok = sem("c_ok")
        ada_used = sem("ada_used")
        ada_pool = sem("ada_pool")
        ada_turned = sem("ada_turned")
        ada_red = sem("ada_red")
        mod_ok = sem("mod_ok")
        x_turned = sem("x_turned")
        x_ok = sem("x_ok")
        sq_ok = sem("sq_ok")
        half_done = sem("half_done")
        half_ok = sem("half_ok")
        sq_half = sem("sq_half")
        ss_ok = sem("ss_ok")
        norm_pe = sem("norm_pe")
        norm_y = sem("norm_y")
        norm_v = sem("norm_v")
        norm_ok = sem("norm_ok")
        hs_ok = sem("hs_ok")
        hh_ok = sem("hh_ok")
        h_ok = sem("h_ok")
        hi_ok = sem("hi_ok")
        lo_ok = sem("lo_ok")
        pe_done = sem("pe_done")
        bank_free = sem("bank_free")
        conv0 = sem("conv0")
        conv1 = sem("conv1")
        conv2 = sem("conv2")
        pad_ok = sem("pad_ok")
        g_hi_ok = sem("g_hi_ok")
        g_a = sem("g_a")
        g_ok = sem("g_ok")
        hn_sq = sem("hn_sq")
        hn_pe = sem("hn_pe")
        hn_y = sem("hn_y")
        hn_v = sem("hn_v")
        normed = sem("normed")
        v_copied = sem("v_copied")
        k_hi_ok = sem("k_hi_ok")
        k_ok = sem("k_ok")
        v_turned = sem("v_turned")
        v_hi_ok = sem("v_hi_ok")
        v_ok = sem("v_ok")
        wf_hi_ok = sem("wf_hi_ok")
        wf_ok = sem("wf_ok")
        wf_zero = sem("wf_zero")
        fg_pe = sem("fg_pe")
        fg_act = sem("fg_act")
        fg_sum = sem("fg_sum")
        fg_ok = sem("fg_ok")
        pads_ok = sem("pads_ok")
        qp_hi = sem("qp_hi")
        qp_ok = sem("qp_ok")
        s_ok = sem("s_ok")
        max_ok = sem("max_ok")
        exp_ok = sem("exp_ok")
        p_ok = sem("p_ok")
        t_ok = sem("t_ok")
        pt_hi_ok = sem("pt_hi_ok")
        pt_ok = sem("pt_ok")
        pv_ok = sem("pv_ok")
        o_hi_ok = sem("o_hi_ok")
        o_ok = sem("o_ok")
        y_turned = sem("y_turned")
        y_ok = sem("y_ok")

        block = ctx.enter_context(nc.Block())

        G_CONV, G_MLP0 = 0, KT
        G_MLP1 = KT + CH * KT
        H_MIX0, H_MLP0, H_KV, H_Q, H_MLP1 = 0, KT, 3 * KT, 5 * KT, 6 * KT
        HALF = [slice(0, T // 2), slice(T // 2, T)]
        ALL = slice(0, T)
        SQ = [0, KT, 2 * KT - 1, 3 * KT - 2]

        def norm_no(n, half):
            return 2 * n - 1 + half if n else 0
        ADA_ORDER = [0, 2, 1, 3] + list(range(4, 2 * NMOD * KT // 4))
        ADA_HALF, ADA_GATE, ADA_MLP, ADA_GATE2, ADA_L1, ADA_ALL = 2, 4, 6, 10, 12, 24
        M_HALF, M_MIX0, M_MLP0, M_MIX1, M_MLP1 = 1, 2, 3, 4, 5
        C_IDENT, C_EPS, C_ONES, C_IDENT_B, C_MASK, C_HEAD, C_PICK, C_NEG_F = 1, 2, 3, 4, 5, 7, 8, 9

        @block.sync
        def _(sp):
            def rows(first, src):
                sp.dma_start(rows_a[first:first + src.shape[0], :], src).then_inc(rows_in, 16)

            rows(R_C, c_in.rearrange("a (k p) -> (a k) p", p=P))
            rows(R_MIX, norm_mix_g.rearrange("l (k p) -> (l k) p", p=P))
            rows(R_MLP, norm_mlp_g.rearrange("l (k p) -> (l k) p", p=P))
            rows(R_CONV, sc_conv.rearrange("a w (k p) -> (a w k) p", p=P))
            rows(R_KV, kv_norm_g.rearrange("(k p) -> k p", p=P))
            for half in range(2):
                sp.dma_start(rows_a[R_KN:R_KN + 1, half * HD:(half + 1) * HD],
                             k_norm_g.rearrange("(a n) -> a n", a=1)).then_inc(rows_in, 16)
                sp.dma_start(rows_a[R_QN:R_QN + 1, half * HD:(half + 1) * HD],
                             q_norm_g).then_inc(rows_in, 16)
            sp.dma_start(rows_b[:], ada_b.rearrange("l (k p) -> (l k) p", p=P)).then_inc(rows_in, 16)
            sp.dma_start(bf_col[:], b_f.rearrange("(h a) -> h a", a=1)).then_inc(rows_in, 16)

            def columns(w, c0=0):
                v = w.rearrange("(k p) n -> p k n", p=P)
                return lambda i: (v[:, :, c0 + i * 2 * P:c0 + (i + 1) * 2 * P] if isinstance(i, int)
                                  else v[:, :, bass.ds(i * (2 * P) + c0, 2 * P)])

            def load_pair(s, source, i):
                sp.dma_start(raw[:, s, :, :], source(i)).then_inc(raw_in[s], 16)

            c_g = columns(sc_w_in[0], D)
            for half in range(2):
                for k in range(KT):
                    if half:
                        sp.wait_ge(ada_used, k + 1)
                    src = ada_w[0, k * P:(k + 1) * P, 0:2 * D].rearrange("p (a b c) -> p a b c", a=2, b=2)
                    sp.dma_start(ada_first[:, k, :, :], src[:, :, half, :]).then_inc(ada_in[k], 16)
                load_pair(half, c_g, half)

            def pairs(first, n, source):
                with sp.Fori(0, n // 2) as i:
                    for s in range(2):
                        sp.wait_ge(lo_ok, 4 * i + 2 * (first + s) - 2)
                        load_pair(s, source, 2 * i + s)

            def mlp(layer, first):
                w1 = mlp_w1[layer].rearrange("(k p) n -> p k n", p=P)
                w2 = mlp_w2[layer].rearrange("(k p) n -> p k n", p=P)
                with sp.Fori(0, CH) as c:
                    pairs(KT * c + first // 2, KT // 2,
                          lambda i: w1[:, :, bass.ds(c * D + i * (2 * P), 2 * P)])
                    pairs(KT * c + (first + KT) // 2, KT // 2,
                          lambda i: w2[:, bass.ds(c * KT, KT), bass.ds(i * (2 * P), 2 * P)])

            for s in range(2):
                sp.wait_ge(lo_ok, 2 * s + 2)
                load_pair(s, c_g, 2 + s)
            pairs(4, 4, columns(sc_w_in[0], 2 * D))
            pairs(8, 4, columns(sc_w_in[0], 0))
            pairs(WOUT // 2, 4, columns(sc_w_out[0]))
            mlp(0, MLP0)
            for (kind, j), b in BLOCK_OF.items():
                half, slot = b % 2, b // 2 % 2
                if half == 0:
                    sp.wait_ge(lo_ok, b - 2)
                src = q_w[0] if kind == "q" else w_kv
                c0 = j * P + (D if kind == "v" else 0)
                sp.dma_start(raw[:, slot, :, half * P:(half + 1) * P],
                             src.rearrange("(k p) n -> p k n", p=P)[:, :, c0:c0 + P]
                             ).then_inc((half_in if half else raw_in)[slot], 16)
            pairs(OUT // 2, 4, columns(o_w[0]))
            mlp(1, MLP1)
            for j in range(KT):
                sp.wait_ge(y_ok, j + 1)
                sp.dma_start(out[0].rearrange("(t p) d -> p t d", p=P)[:, :, j * P:(j + 1) * P],
                             y_rows[:, j, :, :]).then_inc(out_done, 16)
            sp.wait_ge(out_done, 16 * KT)

        @block.gpsimd
        def _(pool):
            steps = [0]

            def link(ins):
                steps[0] += 1
                ins.then_inc(pool_step, 1)
                pool.wait_ge(pool_step, steps[0])

            counted = {}

            def after(ins, signal):
                counted[signal.name] = counted.get(signal.name, 0) + 1
                ins.then_inc(signal, 1)
                pool.wait_ge(signal, counted[signal.name])

            def diagonal(t):
                link(pool.memset(t[:], 0.0))
                after(pool.affine_select(out=t[:], in_=t[:], compare_op=ALU.not_equal, fill=1.0, base=0,
                                         pattern=[[-1, P]], channel_multiplier=1), consts)

            diagonal(ident)
            after(pool.memset(eps_col[:], EPS), consts)
            after(pool.memset(ones[:], 1.0), consts)
            link(pool.memset(ada_acc[:, 2 * D:], 0.0))
            todo = [(0, k, part * D, D) for part in range(2, NMOD) for k in range(KT)]
            todo += [(1, k, part * D, 2 * D) for part in range(0, NMOD, 2) for k in range(KT)]
            last_of_layer_0 = (NMOD - 2) * KT

            def load(i):
                layer, k, c0, n = todo[i]
                if i >= 2:
                    pool.wait_ge(ada_pool, i - 1)
                pool.dma_start(ada_raw[:, i % 2, 0:n],
                               ada_w[layer, k * P:(k + 1) * P, c0:c0 + n]).then_inc(ada_more[i % 2], 16)

            diagonal(ident_b)
            link(pool.memset(mask_b[:], 0.0))
            after(pool.affine_select(out=mask_b[:], in_=mask_b[:], compare_op=ALU.is_ge, fill=MASKED,
                                     base=0, pattern=[[-1, P]], channel_multiplier=1), consts)
            link(pool.memset(ones_head[:], 0.0))
            for half in range(2):
                own = slice(half * HD, (half + 1) * HD)
                after(pool.memset(ones_head[own, own], 1.0), consts)
            link(pool.memset(pick[:], 0.0))
            for part in range(3):
                one = pool.affine_select(out=pick[:], in_=pick[:], compare_op=ALU.not_equal, fill=1.0,
                                         base=-32 * part, pattern=[[-1, HEADS], [0, P]],
                                         channel_multiplier=1)
                if part < 2:
                    link(one)
                else:
                    after(one, consts)
            after(pool.memset(neg_f[:], 0.0), consts)

            pool.wait_ge(c_ok, 1)
            pool.wait_ge(ada_used, KT + KT // 2)
            load(0)
            load(1)
            for i, (layer, k, c0, n) in enumerate(todo):
                if i == last_of_layer_0:
                    pool.wait_ge(ada_turned, ADA_L1)
                    link(pool.memset(ada_acc[:], 0.0))
                if i:
                    pool.wait_ge(ada_pool, i)
                pool.wait_ge(ada_more[i % 2], 16 * (i // 2 + 1))
                acc, part_raw = ada_acc[:, c0:c0 + n], ada_raw[:, i % 2, 0:n]
                link(pool.tensor_tensor(part_raw, part_raw, c_act[:, k:k + 1].to_broadcast([P, n]), ALU.mult))
                pool.tensor_tensor(acc, acc, part_raw, ALU.add).then_inc(ada_pool, 1)
                if i + 2 < len(todo):
                    load(i + 2)

            pool.wait_ge(ada_turned, ADA_ALL)
            pool.dma_start(wf_raw[:], w_f.rearrange("(k p) h -> p k h", p=P)).then_inc(wf_loaded, 16)
            after(pool.memset(wf_hi[:].bitcast(F32), 0.0), wf_zero)
            after(pool.memset(wf_lo[:].bitcast(F32), 0.0), wf_zero)
            for half in range(2):
                other = slice((1 - half) * HD, (2 - half) * HD)
                for t in q_pad[half]:
                    after(pool.memset(t[other, :].bitcast(F32), 0.0), pads_ok)
            after(pool.memset(pt_hi[:, 0, :].bitcast(F32), 0.0), pads_ok)
            after(pool.memset(pt_lo[:, 0, :].bitcast(F32), 0.0), pads_ok)
            f = fg_f[:]
            pool.wait_ge(fg_sum, 1)
            link(pool.tensor_copy(neg_f[0:HEADS, :], f))
            link(pool.tensor_tensor(fg_u[:], f, neg_f[0:HEADS, :], ALU.subtract))
            link(pool.tensor_copy(neg_f[32:32 + HEADS, :], fg_u[:]))
            link(pool.tensor_copy(fg_p[:], fg_u[:]))
            pool.tensor_tensor(neg_f[64:64 + HEADS, :], fg_u[:], fg_p[:], ALU.subtract).then_inc(fg_ok, 1)
        @block.tensor
        def _(pe):
            mm, turn = nc.tensor.matmul, nc.tensor.transpose

            def products(out, weights_hi, weights_lo, hi, lo, k, cols=ALL):
                mm(out[:, cols], weights_hi, hi[:, k, cols], start=(k == 0), stop=False)
                mm(out[:, cols], weights_hi, lo[:, k, cols], start=False, stop=False)
                return mm(out[:, cols], weights_lo, hi[:, k, cols], start=False, stop=(k == KT - 1))

            def part_of(b, s, out, hi, lo, tiles, ready=None, cols=ALL):
                pe.wait_ge(lo_ok, b + 1)
                for k in tiles:
                    if ready:
                        ready(k)
                    last = products(out, w_hi[:, s, k, :], w_lo[:, s, k, :], hi, lo, k, cols)
                return last

            def dense(g, jj, hi, lo, ready=None, between=None):
                if not isinstance(g, int) or g > 0:
                    pe.wait_ge(bank_free, 4 * g + jj - 3)
                b, s, out = 4 * g + jj, jj % 2, bank[jj]
                if between:
                    part_of(b, s, out, hi, lo, range(0, 6), ready)
                    between()
                    last = part_of(b, s, out, hi, lo, range(6, KT), ready)
                else:
                    last = part_of(b, s, out, hi, lo, range(KT), ready)
                last.then_inc(pe_done, 1)

            def layer(first, n, hi, lo, ready):
                with pe.Fori(0, n) as i:
                    for jj in range(GROUP):
                        dense(i + first, jj, hi, lo, ready if jj == 0 else None)

            def norm_sum(n, half):
                out, cols = bank[4 + half][:, 0:T // 2], HALF[half]
                pe.wait_ge(ss_ok, SQ[n] + KT - 1)
                mm(out, ones[:], ssum[:, cols], start=True, stop=False)
                pe.wait_ge(sq_half, norm_no(n, half))
                mm(out, ones[:], tb[:, 1, cols], start=False, stop=True).then_inc(norm_pe, 1)

            def last_block(b, hi, lo, n):
                pe.wait_ge(bank_free, b - 3)
                part_of(b, b % 2, bank[3], hi, lo, range(KT), cols=HALF[0]).then_inc(half_done, 1)
                part_of(b, b % 2, bank[7], hi, lo, range(0, 5), cols=HALF[1])
                norm_sum(n, 0)
                part_of(b, b % 2, bank[7], hi, lo, range(5, KT), cols=HALF[1]).then_inc(pe_done, 1)
                norm_sum(n, 1)

            def first_pair(base, targets):
                def step(which, half, k):
                    out, weights_hi, weights_lo, done, split_at = targets[which]
                    pe.wait_ge(h_ok, base + half * KT + k + 1)
                    if k == 0 and half == 0:
                        pe.wait_ge(*split_at)
                    last = products(out, weights_hi(k), weights_lo(k), h_hi, h_lo, k, HALF[half])
                    if half and k == KT - 1:
                        last.then_inc(done, 1)

                for half, lag in ((0, KT), (1, 3)):
                    for k in range(KT + lag):
                        if k < KT:
                            step(0, half, k)
                        if k >= lag:
                            step(1, half, k - lag)

            def block_target(b, out):
                return out, lambda k: w_hi[:, b % 2, k, :], lambda k: w_lo[:, b % 2, k, :], pe_done, (lo_ok, b + 1)

            def ada_turn(first, last):
                for n in range(first, last):
                    if n >= 4:
                        pe.wait_ge(ada_red, n - 3)
                    for i in range(4):
                        c = (ADA_ORDER[n] % ADA_L1) * 4 + i
                        t = turn(bank[4 + n % 4][:, i * P:(i + 1) * P], ada_acc[:, c * P:(c + 1) * P], ident[:])
                    t.then_inc(ada_turned, 1)

            pe.wait_ge(consts, C_ONES)
            pe.wait_ge(rows_in, 16 * 11)
            turn(bank[7][:, 0:ROWS], rows_a[:], ident[0:ROWS, 0:ROWS]).then_inc(cols_pe, 1)
            nb = 2 * NMOD * KT
            turn(bank[6][:, 0:nb], rows_b[:], ident[0:nb, 0:nb]).then_inc(cols_pe, 1)
            pe.wait_ge(x_loaded, 16)

            def add_square(j):
                pe.wait_ge(sq_ok, j + 1)
                mm(bank[4][:], ones[:], tb[:, j % 2, :], start=(j == 0), stop=(j == KT - 1)).then_inc(ss_ok, 1)

            for j in range(KT):
                if j >= 4:
                    pe.wait_ge(x_ok, j - 3)
                for t in range(TT):
                    v = turn(bank[j % 4][:, t * P:(t + 1) * P], x_rows[:, t, j * P:(j + 1) * P], ident[:])
                v.then_inc(x_turned, 1)
                if j >= 2:
                    add_square(j - 2)
            add_square(KT - 2)
            add_square(KT - 1)
            pe.wait_ge(ada_used, KT)
            pe.wait_ge(norm_v, 1)
            pe.wait_ge(cols_ok, 2)
            ada_turn(0, ADA_HALF)

            pe.wait_ge(x_ok, KT)
            first_h = lambda k: pe.wait_ge(h_ok, H_MIX0 + k + 1)
            for jj in range(2):
                part_of(jj, jj, bank[jj], h_hi, h_lo, range(0, KT // 2), first_h if jj == 0 else None)
            pe.wait_ge(ada_used, 2 * KT)
            ada_turn(ADA_HALF, ADA_GATE)
            for jj in range(2):
                part_of(jj, jj, bank[jj], h_hi, h_lo, range(KT // 2, KT), first_h if jj == 0 else None).then_inc(pe_done, 1)
            for jj in range(2, GROUP):
                dense(0, jj, h_hi, h_lo)
            layer(1, 3 * KT // GROUP - 1, h_hi, h_lo, None)
            pe.wait_ge(ada_pool, KT)
            ada_turn(ADA_GATE, ADA_MLP)
            for jj in range(GROUP):
                dense(WOUT // GROUP, jj, g_hi, g_lo, (lambda k: pe.wait_ge(g_ok, G_CONV + k + 1)) if jj == 0 else None)
            pe.wait_ge(ada_pool, 3 * KT)
            ada_turn(ADA_MLP, ADA_GATE2)
            for jj in range(GROUP - 1):
                dense(WOUT // GROUP + 1, jj, g_hi, g_lo)
            pe.wait_ge(ada_red, ADA_GATE2)
            last_block(WOUT + KT - 1, g_hi, g_lo, 1)

            def mlp(first, h_base, g_base, final):
                def up(c):
                    layer(first // GROUP + 4 * c, 2, h_hi, h_lo, None)

                def down_ready(c):
                    return lambda k: pe.wait_ge(g_ok, g_base + KT * c + k + 1)

                g = first // GROUP
                pe.wait_ge(bank_free, first - 2)
                first_pair(h_base, [block_target(first + i, bank[i]) for i in range(2)])
                for jj in range(2, 2 * GROUP):
                    dense(g + jj // GROUP, jj % GROUP, h_hi, h_lo)
                layer(g + 2, 2, g_hi, g_lo, down_ready(0))
                with pe.Fori(1, CH - 1) as c:
                    up(c)
                    layer(4 * c + (g + 2), 2, g_hi, g_lo, down_ready(c))
                if not final:
                    pe.wait_ge(ada_pool, 7 * KT)
                    ada_turn(ADA_L1, ADA_L1 + 4)
                up(CH - 1)
                ready = down_ready(CH - 1)
                for j in range(KT if final else KT - 1):
                    if not final and j % GROUP == 0:
                        at_group = ADA_L1 + 4 * (j // GROUP + 1)
                        ada_turn(at_group, at_group + 4)
                    dense(g + 4 * (CH - 1) + 2 + j // GROUP, j % GROUP, g_hi, g_lo, ready if j == 0 else None,
                          y_turn(j - 1) if final and j else None)

            def y_turn(j):
                def go():
                    pe.wait_ge(bank_free, BLOCKS - KT + j + 1)
                    if j >= 2:
                        pe.wait_ge(y_ok, j - 1)
                    for t in range(TT):
                        v = turn(bank[4 + j % 2][:, t * P:(t + 1) * P], x[:, j, t * P:(t + 1) * P], ident[:])
                    v.then_inc(y_turned, 1)
                return go

            pe.wait_ge(ada_pool, 4 * KT)
            pe.wait_ge(bank_free, MLP0)
            ada_turn(ADA_GATE2, ADA_L1)
            mlp(MLP0, H_MLP0, G_MLP0, False)
            pe.wait_ge(ada_red, ADA_ALL)
            last_block(KVQ - 1, g_hi, g_lo, 2)

            EARLY, LATE = range(0, KT // 2), range(KT // 2, KT)

            def kvq(kind, j, tiles, ready=None):
                b = BLOCK_OF[kind, j]
                hi, lo = (g_hi, g_lo) if kind == "q" else (h_hi, h_lo)
                last = part_of(b, b % 2, bank[KVQ_BANK[kind, j]], hi, lo, tiles, ready)
                if tiles[-1] == KT - 1:
                    last.then_inc(pe_done, 1)

            def head_sum(kind, j):
                pe.wait_ge(hn_sq, SQUARE_OF[kind, j] + 1)
                mm(bank[SUM_BANK[kind, j]][:], ones_head[:], tb[:, 0 if kind == "q" else 1, :], start=True,
                   stop=True).then_inc(hn_pe, 1)

            def v_turn(j):
                pe.wait_ge(v_copied, j + 1)
                for t in range(TT):
                    v = turn(bank[MISC][:, t * P:(t + 1) * P], tb[:, 0, t * P:(t + 1) * P], ident[:])
                v.then_inc(v_turned, 1)

            def logits(h):
                hi, lo = q_pad[h % 2]
                pe.wait_ge(k_ok, h // 2 + 1)
                pe.wait_ge(qp_ok, h + 1)
                if h:
                    pe.wait_ge(pt_ok, 3 * h)
                for qt in Q_TILES:
                    n = max((qt + 1) * P, 2 * P)
                    q_cols = slice(qt * P, (qt + 1) * P)
                    at_bank, c0 = LOGITS_AT[qt]
                    o = bank[at_bank][:, c0:c0 + n]
                    mm(o, hi[:, q_cols], k_hi[:, 0:n], start=True, stop=False)
                    mm(o, hi[:, q_cols], k_lo[:, 0:n], start=False, stop=False)
                    mm(bank[at_bank][:, c0 + qt * P:c0 + (qt + 1) * P], ident_b[:], mask_b[:], start=False,
                       stop=False, skip_group_check=True)
                    mm(o, lo[:, q_cols], k_hi[:, 0:n], start=False, stop=False)
                    mm(o, pick[:, h, :], neg_f[:, 0:n], start=False, stop=True).then_inc(s_ok, 1)

            def turn_probs(h):
                pe.wait_ge(p_ok, h + 1)
                for i, tiles in enumerate(((0,), (1, 3), (2,))):
                    at_col = 0
                    for kt in tiles:
                        for qt in range(kt, TT):
                            v = turn(bank[4 + i][:, at_col:at_col + P],
                                     probs[:, P_OFF[qt] + kt * P:P_OFF[qt] + (kt + 1) * P], ident[:])
                            at_col += P
                    v.then_inc(t_ok, 1)

            def output(h):
                pe.wait_ge(v_ok, h // 2 + 1)
                pe.wait_ge(pt_ok, 3 * (h + 1))
                if h:
                    pe.wait_ge(o_ok, h)

                def prob_t(t, kt):
                    return (t[:, PT_AT[kt]:PT_AT[kt] + TT - kt, :] if kt < 3
                            else t[:, 0:PT_AT[3] + 1:PT_AT[3], :])

                def add(v, kt, t, first=False, end=False):
                    return mm(bank[7][:, min(kt, 2) * P:T], v[:, kt, :], prob_t(t, kt),
                              start=first, stop=end, skip_group_check=True)

                add(v_hi, 0, pt_hi, first=True)
                for kt in range(1, TT):
                    add(v_hi, kt, pt_hi)
                    add(v_hi, kt, pt_lo)
                    add(v_lo, kt, pt_hi)
                add(v_hi, 0, pt_lo)
                last = add(v_lo, 0, pt_hi, end=True)
                last.then_inc(pv_ok, 1)

            pe.wait_ge(consts, C_NEG_F)
            pe.wait_ge(bank_free, KVQ - 2)
            first_pair(H_KV, [(bank[6], lambda k: wf_hi[:, k, :], lambda k: wf_lo[:, k, :], fg_pe, (wf_ok, 1)),
                              block_target(KVQ, bank[KVQ_BANK["k", 0]])])
            pe.wait_ge(bank_free, KVQ)
            kvq("v", 0, EARLY)
            head_sum("k", 0)
            kvq("v", 0, LATE)
            kvq("k", 1, range(KT))
            kvq("q", 0, EARLY, lambda k: pe.wait_ge(h_ok, H_Q + k + 1))
            pe.wait_ge(hn_v, 1)
            v_turn(0)
            kvq("q", 0, LATE, lambda k: pe.wait_ge(h_ok, H_Q + k + 1))
            head_sum("q", 0)
            pe.wait_ge(fg_ok, 1)
            pe.wait_ge(pads_ok, 6)
            pe.wait_ge(hn_v, NORM_OF["q", 0] + 1)
            def project(n, tiles):
                last = part_of(OUT + n, n, bank[n], o_hi, o_lo, tiles, lambda k: pe.wait_ge(o_ok, 2 * k + 2))
                if tiles[-1] == KT - 1:
                    last.then_inc(pe_done, 1)

            for i in range(KT):
                nxt = i + 1
                q_cut, v_cut = (6, 3) if i else (3, 6)
                logits(2 * i)
                if i:
                    output(2 * i - 1)
                    pe.wait_ge(hn_v, 2 * i + 2)
                    v_turn(i)
                else:
                    pe.wait_ge(v_ok, 1)
                    head_sum("k", 1)
                if nxt == KT:
                    break
                pe.wait_ge(normed, 2 * nxt)
                pe.wait_ge(v_copied, nxt)
                kvq("q", nxt, range(0, q_cut))
                turn_probs(2 * i)
                kvq("q", nxt, range(q_cut, KT))
                if i:
                    kvq("k", nxt, range(0, 2))
                pe.wait_ge(v_ok, nxt)
                pe.wait_ge(hn_v, NORM_OF["q", nxt])
                head_sum("q", nxt)
                if i:
                    kvq("k", nxt, range(2, KT))
                logits(2 * i + 1)
                if i:
                    pe.wait_ge(hn_v, NORM_OF["k", nxt])
                    head_sum("k", nxt)
                else:
                    pe.wait_ge(normed, NORM_OF["k", 1] + 1)
                output(2 * i)
                kvq("v", nxt, range(0, v_cut))
                turn_probs(2 * i + 1)
                kvq("v", nxt, range(v_cut, KT))

            pe.wait_ge(normed, 2 * KT)
            project(0, range(0, 2))
            turn_probs(HEADS - 2)
            project(0, range(2, 6))
            logits(HEADS - 1)
            output(HEADS - 2)
            project(1, range(0, 2))
            turn_probs(HEADS - 1)
            project(0, range(6, 7))
            project(1, range(2, 4))
            output(HEADS - 1)
            project(1, range(4, 5))
            project(0, range(7, KT))
            project(1, range(5, KT))
            pe.wait_ge(bank_free, OUT)
            pe.wait_ge(v_ok, KT)
            for j in range(2, KT - 1):
                dense(OUT // GROUP + j // GROUP, j % GROUP, o_hi, o_lo)
            last_block(OUT + KT - 1, o_hi, o_lo, 3)
            mlp(MLP1, H_MLP1, G_MLP1, True)
            y_turn(KT - 1)()

        @block.scalar
        def _(act):
            steps = [0]
            go = nc.scalar.activation

            def link(ins):
                steps[0] += 1
                ins.then_inc(act_step, 1)
                act.wait_ge(act_step, steps[0])

            def split(g, jj):
                g, jj = g + jj // GROUP, jj % GROUP
                s, pair = jj % 2, jj // 2
                if isinstance(g, int) and 4 * g + jj in BLOCK_OF.values() and s:
                    act.wait_ge(half_in[pair], 16 * (g - KVQ // 4) + 16)
                else:
                    act.wait_ge(raw_in[pair], 16 * g + 16)
                if not isinstance(g, int) or 4 * g + jj >= 2:
                    act.wait_ge(pe_done, 4 * g + jj - 1)
                go(w_hi[:, s, :, :], raw[:, pair, :, s * P:(s + 1) * P], ACT.Copy).then_inc(hi_ok, 1)

            def groups(first, n, step, written_out=False):
                if written_out:
                    for j in range(n * GROUP):
                        step(first + j // GROUP, j % GROUP, j)
                    return
                with act.Fori(0, n) as i:
                    for jj in range(GROUP):
                        step(i + first, jj, 4 * i + jj)

            def square_tile(m, j, s):
                if not isinstance(m, int) or m >= 2:
                    act.wait_ge(ss_ok, m - 1)
                go(tb[:, s, :], tile3(x, j), ACT.Square).then_inc(sq_ok, 1)

            def norm_root(n, half, cols):
                if n:
                    act.wait_ge(norm_pe, norm_no(n, half))
                else:
                    act.wait_ge(ss_ok, KT)
                sums = bank[4 + half][:, 0:cols.stop - cols.start]
                link(go(ty[:, 0, cols], sums, ACT.Ln, bias=eps_col[:], scale=1.0 / D))
                go(ty[:, 0, cols], ty[:, 0, cols], ACT.Exp, scale=-0.5).then_inc(norm_y, 1)
                go(tc[:, 0, cols], sums, ACT.Identity, bias=eps_col[:], scale=1.0 / D).then_inc(norm_v, 1)

            def h_tile(m, j, hi, shift, cols=ALL):
                act.wait_ge(hs_ok, m + 1)
                if shift is None:
                    go(hi[:, j, cols], hs_slot(j, cols), ACT.Copy).then_inc(hh_ok, 1)
                else:
                    go(hi[:, j, cols], hs_slot(j, cols), ACT.Identity, bias=shift).then_inc(hh_ok, 1)

            def last_square(n, half, b):
                if half == 0:
                    act.wait_ge(half_ok, n)
                    act.wait_ge(ss_ok, SQ[n] + KT - 2)
                else:
                    act.wait_ge(bank_free, b + 1)
                go(tb[:, 1, HALF[half]], x[:, KT - 1, HALF[half]], ACT.Square).then_inc(sq_half, 1)

            def norm_in_halves(n, b, base, shift):
                last_square(n, 0, b)
                norm_root(n, 0, HALF[0])
                last_square(n, 1, b)
                for m in range(2 * KT):
                    if m == 2:
                        norm_root(n, 1, HALF[1])
                    if m == KT:
                        split((b + 2) // GROUP, (b + 2) % GROUP)
                    j = m % KT
                    h_tile(base + m, j, h_hi, shift(j), HALF[m // KT])

            act.dma_start(x_rows[:], x_in[0].rearrange("(t p) d -> p t d", p=P)).then_inc(x_loaded, 16)
            nc.scalar.preload_act_table_set("natural_log_exp_and_others")
            act.wait_ge(cols_ok, 1)
            go(c_tmp[:], cols[:, R_C:R_C + KT], ACT.Exp, scale=-1.0).then_inc(silu_e, 1)
            for j in range(KT):
                act.wait_ge(x_turned, j + 1)
                go(x[:, j, :], bank[j % 4][:], ACT.Copy).then_inc(x_ok, 1)
                act.wait_ge(x_ok, j + 1)
                square_tile(j, j, j % 2)
            act.wait_ge(consts, C_EPS)
            norm_root(0, 0, ALL)
            for jj in range(2):
                split(0, jj)
            for j in range(KT):
                if j % (KT // 2) == 0:
                    act.wait_ge(mod_ok, M_HALF if j == 0 else M_MIX0)
                h_tile(H_MIX0 + j, j, h_hi, mcol(0, 0, j))

            def step_cg(g, jj, j):
                split(g, jj + 2)
                act.wait_ge(pe_done, 4 * g + jj + 1)
                go(z[:, bass.ds(j, 1), CONV - 1:] if not isinstance(j, int) else z[:, j:j + 1, CONV - 1:],
                   bank[jj][:].rearrange("p (a t) -> p a t", a=1), ACT.Copy).then_inc(bank_free, 1)

            def step_xv(g, jj, j):
                split(g, jj + 2)

            def step_bg(g, jj, j):
                act.wait_ge(bank_free, 4 * g + jj - 1)
                z_t = z[:, bass.ds(j, 1), CONV - 1:] if not isinstance(j, int) else z[:, j:j + 1, CONV - 1:]
                go(ta[:, jj % 2, :].rearrange("p (a t) -> p a t", a=1), z_t, ACT.Copy,
                   scale=col(cols, j + (R_CONV + 2 * KT))).then_inc(conv0, 1)
                split(g, jj + 2)
                act.wait_ge(bank_free, 4 * g + jj + 1)
                go(tile3(g_hi, j), tb[:, jj % 2, :], ACT.Copy).then_inc(g_hi_ok, 1)

            groups(WIN // GROUP, 2, step_cg)
            groups(WIN // GROUP + 2, 2, step_xv)
            groups(WIN // GROUP + 4, 2, step_bg)

            def step_proj(base=None):
                def step(g, jj, j):
                    if not (isinstance(j, int) and j == KT - 2):
                        split(g, jj + 2)
                    act.wait_ge(bank_free, 4 * g + jj + 1)
                    square_tile(j + base, j, jj % 2)
                    if isinstance(j, int) and j == KT - 2:
                        split(g, jj + 2)
                return step

            act.wait_ge(g_ok, G_CONV + KT)

            def into_stream(first, n):
                for j in range(KT - 1):
                    step_proj(SQ[n])(first // GROUP + j // GROUP, j % GROUP, j)
                if n == 2:
                    act.wait_ge(wf_loaded, 16)
                    act.wait_ge(wf_zero, 2)
                    go(wf_hi[:, :, 0:HEADS], wf_raw[:], ACT.Copy).then_inc(wf_hi_ok, 1)

            into_stream(WOUT, 1)
            act.wait_ge(mod_ok, M_MLP0)
            norm_in_halves(1, WOUT + KT - 1, H_MLP0, lambda j: mcol(0, 3, j))

            def mlp(first, g_base, final):
                def step_up(c):
                    def step(g, jj, j):
                        split(g, jj + 2)
                        act.wait_ge(pe_done, 4 * g + jj + 1)
                        act.wait_ge(bank_free, 4 * g + jj)
                        act.wait_ge(g_ok, KT * c + j + (g_base - 1))
                        go(ta[:, jj % 2, :], bank[jj][:], ACT.Relu).then_inc(bank_free, 1)
                        act.wait_ge(bank_free, 4 * g + jj + 1)
                        go(tile3(g_hi, j), ta[:, jj % 2, :], ACT.Square).then_inc(g_hi_ok, 1)
                    return step

                def step_down(g, jj, j):
                    split(g, jj + 2)

                def step_final(g, jj, j):
                    if j < KT - 2:
                        split(g, jj + 2)
                    if j:
                        y_tile(j - 1)

                def y_tile(j):
                    act.wait_ge(y_turned, j + 1)
                    go(y_rows[:, j, :, :], bank[4 + j % 2][:].rearrange("p (t f) -> p t f", f=P),
                       ACT.Copy).then_inc(y_ok, 1)

                g0 = first // GROUP
                with act.Fori(0, CH - 1) as c:
                    groups(4 * c + g0, 2, step_up(c))
                    groups(4 * c + (g0 + 2), 2, step_down)
                c = CH - 1
                groups(4 * c + g0, 2, step_up(c))
                act.wait_ge(g_ok, g_base + KT * CH)
                if final:
                    groups(4 * c + g0 + 2, 2, step_final, True)
                    y_tile(KT - 1)
                else:
                    into_stream(first + (2 * CH - 1) * KT, 2)

            mlp(MLP0, G_MLP0, False)
            norm_in_halves(2, KVQ - 1, H_KV, lambda j: None)
            def forget_gate():
                act.wait_ge(fg_pe, 1)
                go(fg_u[:], bank[6][0:HEADS, :], ACT.Identity, bias=bf_col[:]).then_inc(fg_act, 1)
                link(go(fg_l[:], bank[6][0:HEADS, :], ACT.Abs, bias=bf_col[:]))
                link(go(fg_l[:], fg_l[:], ACT.Exp, scale=-1.0))
                go(fg_l[:], fg_l[:], ACT.Ln, bias=ones[0:HEADS, 0:1]).then_inc(fg_act, 1)

            def after_block(kind, j):
                b = BLOCK_OF[kind, j] + 2
                split(b // GROUP, b % GROUP)

            def head_square(kind, j):
                act.wait_ge(pe_done, BLOCK_OF[kind, j] + 1)
                if kind == "q":
                    act.wait_ge(v_turned, max(j, 1))
                elif j:
                    act.wait_ge(hn_pe, NORM_OF["k", j - 1] + 1)
                go(tb[:, 0 if kind == "q" else 1, :], bank[KVQ_BANK[kind, j]][:], ACT.Square).then_inc(hn_sq, 1)

            def head_root(kind, j):
                act.wait_ge(hn_pe, NORM_OF[kind, j] + 1)
                if kind == "q":
                    if j:
                        act.wait_ge(qp_ok, 2 * j)
                elif j:
                    act.wait_ge(k_ok, j)
                v, y = (tc[:, 0, :], ty[:, 0, :]) if kind == "q" else (tv[:], ty[:, 1, :])
                link(go(y, bank[SUM_BANK[kind, j]][:], ACT.Ln, bias=eps_col[:], scale=1.0 / HD))
                go(y, y, ACT.Exp, scale=-0.5).then_inc(hn_y, 1)
                go(v, bank[SUM_BANK[kind, j]][:], ACT.Identity, bias=eps_col[:], scale=1.0 / HD).then_inc(hn_v, 1)

            def k_high(j):
                act.wait_ge(normed, NORM_OF["k", j] + 1)
                if j:
                    act.wait_ge(s_ok, 2 * TT * j)
                go(k_hi[:], ty[:, 1, :], ACT.Copy).then_inc(k_hi_ok, 1)

            def v_copy(j):
                act.wait_ge(pe_done, BLOCK_OF["v", j] + 1)
                if j:
                    act.wait_ge(hn_pe, NORM_OF["q", j] + 1)
                go(tb[:, 0, :], bank[KVQ_BANK["v", j]][:], ACT.Copy).then_inc(v_copied, 1)

            def v_high(j):
                act.wait_ge(v_turned, j + 1)
                if j:
                    act.wait_ge(pv_ok, 2 * j)
                go(v_hi[:], bank[MISC][:].rearrange("p (t f) -> p t f", f=P), ACT.Copy).then_inc(v_hi_ok, 1)

            def q_high(h):
                half = h % 2
                own = slice(half * HD, (half + 1) * HD)
                act.wait_ge(normed, NORM_OF["q", h // 2] + 1)
                if h >= 2:
                    act.wait_ge(s_ok, TT * (h - 1))
                go(q_pad[half][0][own, :], ty[own, 0, :], ACT.Copy).then_inc(qp_hi, 1)

            def exponentials(h):
                for i, qt in enumerate(Q_TILES):
                    s = TT * (h % 2) + i
                    n = (qt + 1) * P
                    at_bank, c0 = LOGITS_AT[qt]
                    act.wait_ge(max_ok, TT * h + (i + 1 if i < 2 else TT))
                    if i == 0 and h:
                        act.wait_ge(t_ok, 3 * h)
                        act.wait_ge(p_ok, h)
                    go(probs[:, P_OFF[qt]:P_OFF[qt] + n], bank[at_bank][:, c0:c0 + n], ACT.Exp,
                       bias=neg_max[:, s:s + 1], accum_out=p_sum[:, s:s + 1]).then_inc(exp_ok, 1)

            def probs_high(h):
                for i in range(3):
                    act.wait_ge(t_ok, 3 * h + i + 1)
                    if h:
                        act.wait_ge(pv_ok, h)
                    first, n = ((1, 4), (5, 4), (9, 2))[i]
                    go(pt_hi[:, first:first + n, :],
                       bank[4 + i][:, 0:n * P].rearrange("p (b c) -> p b c", c=P),
                       ACT.Copy).then_inc(pt_hi_ok, 1)

            def out_high(h):
                own = slice((h % 2) * HD, (h % 2 + 1) * HD)
                act.wait_ge(pv_ok, h + 1)
                go(o_hi[own, h // 2, :], bank[7][own, :], ACT.Copy).then_inc(o_hi_ok, 1)

            act.wait_ge(norm_pe, norm_no(2, 1))
            act.wait_ge(mod_ok, M_MIX1)

            def query_input(first, last):
                for j in range(first, last):
                    h_tile(H_Q + j, j, g_hi, mcol(1, 0, j))

            head_square("k", 0)
            after_block("k", 0)
            forget_gate()
            query_input(0, KT // 2)
            head_root("k", 0)
            v_copy(0)
            after_block("v", 0)
            query_input(KT // 2, KT)
            k_high(0)
            head_square("k", 1)
            after_block("k", 1)
            head_square("q", 0)
            head_root("q", 0)
            v_high(0)
            q_high(0)
            q_high(1)
            after_block("q", 0)
            for i in range(KT):
                nxt = i + 1
                exponentials(2 * i)
                if i:
                    out_high(2 * i - 1)
                    v_high(i)
                    after_block("v", i)
                else:
                    head_root("k", 1)
                probs_high(2 * i)
                if nxt < KT:
                    head_square("q", nxt)
                    after_block("q", nxt)
                    head_root("q", nxt)
                    if i:
                        head_square("k", nxt)
                exponentials(2 * i + 1)
                if i and nxt < KT:
                    head_root("k", nxt)
                out_high(2 * i)
                if nxt < KT:
                    q_high(2 * nxt)
                probs_high(2 * i + 1)
                if nxt < KT:
                    k_high(nxt)
                    if i:
                        after_block("k", nxt)
                    q_high(2 * nxt + 1)
                    v_copy(nxt)
            out_high(HEADS - 1)

            into_stream(OUT, 3)
            norm_in_halves(3, OUT + KT - 1, H_MLP1, lambda j: mcol(1, 3, j))
            mlp(MLP1, G_MLP1, True)

        @block.vector
        def _(dve):
            steps = [0]
            tt, stt, ts = nc.vector.tensor_tensor, nc.vector.scalar_tensor_tensor, nc.vector.tensor_scalar

            def link(ins):
                steps[0] += 1
                ins.then_inc(vec_step, 1)
                dve.wait_ge(vec_step, steps[0])

            def split(g, jj):
                g, jj = g + jj // GROUP, jj % GROUP
                s, pair = jj % 2, jj // 2
                dve.wait_ge(hi_ok, 4 * g + jj + 1)
                tt(w_lo[:, s, :, :], raw[:, pair, :, s * P:(s + 1) * P], w_hi[:, s, :, :],
                   ALU.subtract).then_inc(lo_ok, 1)

            def groups(first, n, step, written_out=False, j0=0):
                if written_out:
                    for j in range(n * GROUP):
                        step(first + j // GROUP, j % GROUP, j0 + j)
                    return
                with dve.Fori(0, n) as i:
                    for jj in range(GROUP):
                        step(i + first, jj, 4 * i + jj)

            def add_square(m, s):
                dve.wait_ge(sq_ok, m + 1)
                dve.wait_ge(ss_ok, m)
                tt(ssum[:], ssum[:], tb[:, s, :], ALU.add).then_inc(ss_ok, 1)

            def refine_start(dst, y):
                link(stt(out=dst, in0=y, scalar=-0.5, in1=y, op0=ALU.mult, op1=ALU.mult))

            def refine_end(dst, v, y):
                link(tt(dst, dst, v, ALU.mult))
                link(stt(out=dst, in0=dst, scalar=1.5, in1=y, op0=ALU.add, op1=ALU.mult))

            def norm_end(n, half, cols):
                dve.wait_ge(norm_y, norm_no(n, half) + 1)
                refine_start(rms[:, cols], ty[:, 0, cols])
                dve.wait_ge(norm_v, norm_no(n, half) + 1)
                refine_end(rms[:, cols], tc[:, 0, cols], ty[:, 0, cols])

            def scaled(m, j, gain, cols=ALL):
                if m >= 4:
                    dve.wait_ge(h_ok, m - 3)
                stt(out=hs_slot(j, cols), in0=x[:, j, cols], scalar=gain(j), in1=rms[:, cols], op0=ALU.mult,
                    op1=ALU.mult).then_inc(hs_ok, 1)

            def h_low(m, j, shift, hi, lo, cols=ALL):
                dve.wait_ge(hh_ok, m + 1)
                if shift is None:
                    tt(lo[:, j, cols], hs_slot(j, cols), hi[:, j, cols], ALU.subtract).then_inc(h_ok, 1)
                else:
                    stt(out=lo[:, j, cols], in0=hs_slot(j, cols), scalar=shift(j), in1=hi[:, j, cols],
                        op0=ALU.add, op1=ALU.subtract).then_inc(h_ok, 1)

            def make_h(base, n, shift, hi, lo, first=0, last=KT):
                gain = lambda j: gains[:, n, j:j + 1]
                scaled(base + first, first, gain)
                scaled(base + first + 1, first + 1, gain)
                for j in range(first, last):
                    h_low(base + j, j, shift, hi, lo)
                    if j + 2 < last:
                        scaled(base + j + 2, j + 2, gain)

            def last_tile(half, b, layer, part):
                cols = HALF[half]
                if half == 0:
                    dve.wait_ge(half_done, half_count[0] + 1)
                    half_count[0] += 1
                else:
                    dve.wait_ge(pe_done, b + 1)
                    dve.wait_ge(bank_free, b)
                stt(out=x[:, KT - 1, cols], in0=bank[7 if half else 3][:, cols], scalar=mcol(layer, part, KT - 1),
                    in1=x[:, KT - 1, cols], op0=ALU.mult, op1=ALU.add).then_inc(bank_free if half else half_ok, 1)

            def norm_in_halves(n, b, base, layer, part, gain, shift):
                last_tile(0, b, layer, part)
                norm_end(n, 0, HALF[0])
                last_tile(1, b, layer, part)
                for m in range(2):
                    scaled(base + m, m, gain, HALF[0])
                for m in range(2 * KT):
                    h_low(base + m, m % KT, shift, h_hi, h_lo, HALF[m // KT])
                    if m == 3:
                        norm_end(n, 1, HALF[1])
                    if m + 2 < 2 * KT:
                        scaled(base + m + 2, (m + 2) % KT, gain, HALF[(m + 2) // KT])
                    if m == KT - 1:
                        split((b + 2) // GROUP, (b + 2) % GROUP)

            half_count = [0]

            def ada_reduce(first, last):
                for n in range(first, last):
                    g = ADA_ORDER[n]
                    dve.wait_ge(ada_turned, n + 1)
                    nc.vector.tensor_reduce(mod[:, 4 * g:4 * g + 4], bank[4 + n % 4][:].rearrange("p (a b) -> p a b", b=P),
                                            AX_X, ALU.add).then_inc(ada_red, 1)
                dve.wait_ge(ada_red, last)
                for n in range(first, last):
                    part = slice(4 * ADA_ORDER[n], 4 * ADA_ORDER[n] + 4)
                    done = tt(mod[:, part], mod[:, part], ada_bias[:, part], ALU.add)
                link(done)

            def gain(n, layer, part, row, count, tiles=(0, KT)):
                k = (layer * NMOD + part) * KT
                stt(out=gains[:, n, tiles[0]:tiles[1]], in0=mod[:, k + tiles[0]:k + tiles[1]], scalar=1.0,
                    in1=cols[:, row + tiles[0]:row + tiles[1]], op0=ALU.add, op1=ALU.mult).then_inc(mod_ok, 1)
                dve.wait_ge(mod_ok, count)

            def ada_first_step(half, k):
                n = half * KT + k
                dve.wait_ge(ada_in[k], 16 * (half + 1))
                acc = ada_acc[:, 0:2 * D].rearrange("p (a b c) -> p a b c", a=2, b=2)[:, :, half, :]
                if k == 0:
                    one = ts(acc, ada_first[:, k, :, :], c_act[:, 0:1], None, ALU.mult)
                else:
                    dve.wait_ge(ada_used, n)
                    one = stt(out=acc, in0=ada_first[:, k, :, :], scalar=c_act[:, k:k + 1], in1=acc,
                              op0=ALU.mult, op1=ALU.add)
                one.then_inc(ada_used, 1)

            dve.wait_ge(cols_pe, 1)
            nc.vector.tensor_copy(cols[:], bank[7][:, 0:ROWS]).then_inc(cols_ok, 1)
            dve.wait_ge(cols_pe, 2)
            nc.vector.tensor_copy(ada_bias[:], bank[6][:, 0:2 * NMOD * KT]).then_inc(cols_ok, 1)
            dve.wait_ge(silu_e, 1)
            dve.wait_ge(cols_ok, 2)
            link(ts(c_tmp[:], c_tmp[:], 1.0, None, ALU.add))
            link(nc.vector.reciprocal(c_tmp[:], c_tmp[:]))
            tt(c_act[:], cols[:, R_C:R_C + KT], c_tmp[:], ALU.mult).then_inc(c_ok, 1)
            link(ts(q_gain[:], cols[:, R_QN:R_QN + 1], HD ** -0.5, None, ALU.mult))
            link(nc.vector.memset(ssum[:], 0.0))
            dve.wait_ge(c_ok, 1)
            for j in range(KT):
                ada_first_step(0, j)
            norm_end(0, 0, ALL)
            dve.wait_ge(x_turned, KT)
            link(nc.vector.memset(z[:, :, 0:CONV - 1], 0.0))
            ada_reduce(0, ADA_HALF)
            gain(0, 0, 1, R_MIX, M_HALF, (0, KT // 2))
            split(0, 0)
            make_h(H_MIX0, 0, lambda j: mcol(0, 0, j), h_hi, h_lo, 0, KT // 2)
            split(0, 1)
            for k in range(KT):
                ada_first_step(1, k)
            ada_reduce(ADA_HALF, ADA_GATE)
            gain(0, 0, 1, R_MIX, M_MIX0, (KT // 2, KT))
            make_h(H_MIX0, 0, lambda j: mcol(0, 0, j), h_hi, h_lo, KT // 2, KT)

            def step_cg(g, jj, j):
                split(g, jj + 2)

            def step_xv(g, jj, j):
                split(g, jj + 2)
                dve.wait_ge(pe_done, 4 * g + jj + 1)
                dve.wait_ge(bank_free, 4 * g + jj)
                z_t = z[:, bass.ds(j, 1), CONV - 1:]
                tt(z_t, bank[jj][:].rearrange("p (a t) -> p a t", a=1), z_t, ALU.mult).then_inc(bank_free, 1)

            def step_bg(g, jj, j):
                s = jj % 2
                acc = ta[:, s, :].rearrange("p (a t) -> p a t", a=1)
                dve.wait_ge(conv0, j + 1)
                stt(out=acc, in0=z[:, bass.ds(j, 1), 1:T + 1], scalar=col(cols, j + (R_CONV + KT)), in1=acc,
                    op0=ALU.mult, op1=ALU.add).then_inc(conv1, 1)
                dve.wait_ge(conv1, j + 1)
                stt(out=acc, in0=z[:, bass.ds(j, 1), 0:T], scalar=col(cols, j + R_CONV), in1=acc,
                    op0=ALU.mult, op1=ALU.add).then_inc(conv2, 1)
                split(g, jj + 2)
                dve.wait_ge(pe_done, 4 * g + jj + 1)
                dve.wait_ge(conv2, j + 1)
                tt(tb[:, s, :], bank[jj][:], ta[:, s, :], ALU.mult).then_inc(bank_free, 1)
                dve.wait_ge(g_hi_ok, j + 1)
                dve.wait_ge(bank_free, 4 * g + jj + 1)
                tt(tile3(g_lo, j), tb[:, s, :], tile3(g_hi, j), ALU.subtract).then_inc(g_ok, 1)

            groups(WIN // GROUP, 2, step_cg)
            groups(WIN // GROUP + 2, 2, step_xv)
            groups(WIN // GROUP + 4, 2, step_bg)

            def step_proj(layer, part, base):
                def step(g, jj, j):
                    before_norm = base and isinstance(j, int) and j == KT - 2
                    if not before_norm:
                        split(g, jj + 2)
                    dve.wait_ge(pe_done, 4 * g + jj + 1)
                    dve.wait_ge(bank_free, 4 * g + jj)
                    stt(out=tile3(x, j), in0=bank[jj][:], scalar=mcol(layer, part, j), in1=tile3(x, j),
                        op0=ALU.mult, op1=ALU.add).then_inc(bank_free, 1)
                    if base:
                        add_square(j + base, jj % 2)
                    if before_norm:
                        split(g, jj + 2)
                return step

            ada_reduce(ADA_GATE, ADA_MLP)
            link(nc.vector.memset(ssum[:], 0.0))

            def into_stream(first, n, layer, part, before_second_group=None):
                for j in range(KT - 1):
                    if j == GROUP and before_second_group:
                        before_second_group()
                    step_proj(layer, part, SQ[n])(first // GROUP + j // GROUP, j % GROUP, j)
                if n == 2:
                    dve.wait_ge(wf_hi_ok, 1)
                    tt(wf_lo[:, :, 0:HEADS], wf_raw[:], wf_hi[:, :, 0:HEADS], ALU.subtract).then_inc(wf_ok, 1)

            def mlp_gain():
                ada_reduce(ADA_MLP, ADA_GATE2)
                gain(1, 0, 4, R_MLP, M_MLP0)

            into_stream(WOUT, 1, 0, 2, mlp_gain)
            norm_in_halves(1, WOUT + KT - 1, H_MLP0, 0, 2, lambda j: gains[:, 1, j:j + 1], lambda j: mcol(0, 3, j))
            ada_reduce(ADA_GATE2, ADA_L1)

            def mlp(layer, first, g_base, final):
                def step_up(c):
                    def step(g, jj, j):
                        s = jj % 2
                        split(g, jj + 2)
                        dve.wait_ge(bank_free, 4 * g + jj + 1)
                        tt(tb[:, s, :], ta[:, s, :], ta[:, s, :], ALU.mult).then_inc(g_a, 1)
                        dve.wait_ge(g_a, KT * c + j + (g_base - KT + 1))
                        dve.wait_ge(g_hi_ok, KT * c + j + (g_base + 1))
                        tt(tile3(g_lo, j), tb[:, s, :], tile3(g_hi, j), ALU.subtract).then_inc(g_ok, 1)
                    return step

                def step_final(g, jj, j):
                    if j < KT - 2:
                        split(g, jj + 2)
                    dve.wait_ge(pe_done, 4 * g + jj + 1)
                    dve.wait_ge(bank_free, 4 * g + jj)
                    stt(out=x[:, j, :], in0=bank[jj][:], scalar=mcol(layer, 5, j), in1=x[:, j, :],
                        op0=ALU.mult, op1=ALU.add).then_inc(bank_free, 1)

                g0 = first // GROUP
                with dve.Fori(0, CH - 1) as c:
                    groups(4 * c + g0, 2, step_up(c))
                    groups(4 * c + (g0 + 2), 2, step_proj(layer, 5, None))
                c = CH - 1
                if final:
                    groups(4 * c + g0, 2, step_up(c))
                    groups(4 * c + g0 + 2, 2, step_final, True)
                    return
                ada_reduce(ADA_L1, ADA_L1 + 4)
                gain(2, 1, 1, R_MIX + KT, M_MIX1)
                link(nc.vector.memset(ssum[:], 0.0))
                groups(4 * c + g0, 2, step_up(c))
                ada_reduce(ADA_L1 + 4, ADA_L1 + 8)

                def rest():
                    ada_reduce(ADA_L1 + 8, ADA_ALL)
                    gain(3, 1, 4, R_MLP + KT, M_MLP1)

                into_stream(first + (2 * CH - 1) * KT, 2, layer, 5, rest)

            mlp(0, MLP0, G_MLP0, False)
            norm_in_halves(2, KVQ - 1, H_KV, 0, 5, lambda j: cols[:, R_KV + j:R_KV + j + 1], None)

            def after_block(kind, j):
                b = BLOCK_OF[kind, j] + 2
                split(b // GROUP, b % GROUP)

            def root_of(kind):
                return (tc[:, 0, :], ty[:, 0, :]) if kind == "q" else (tv[:], ty[:, 1, :])

            def head_norm(kind, j):
                v, y = root_of(kind)
                n = NORM_OF[kind, j]
                dve.wait_ge(hn_y, n + 1)
                if n:
                    dve.wait_ge(normed, n)
                refine_start(ssum[:], y)
                dve.wait_ge(hn_v, n + 1)
                refine_end(ssum[:], v, y)
                stt(out=y, in0=bank[KVQ_BANK[kind, j]][:], scalar=q_gain[:] if kind == "q" else cols[:, R_KN:R_KN + 1],
                    in1=ssum[:], op0=ALU.mult, op1=ALU.mult).then_inc(normed, 1)

            def k_low(j):
                dve.wait_ge(k_hi_ok, j + 1)
                tt(k_lo[:], ty[:, 1, :], k_hi[:], ALU.subtract).then_inc(k_ok, 1)

            def v_low(j):
                dve.wait_ge(v_hi_ok, j + 1)
                tt(v_lo[:], bank[MISC][:].rearrange("p (t f) -> p t f", f=P), v_hi[:],
                   ALU.subtract).then_inc(v_ok, 1)

            def q_low(h):
                own = slice((h % 2) * HD, (h % 2 + 1) * HD)
                hi, lo = q_pad[h % 2]
                dve.wait_ge(qp_hi, h + 1)
                tt(lo[own, :], ty[own, 0, :], hi[own, :], ALU.subtract).then_inc(qp_ok, 1)

            def softmax(h):
                slots = slice(TT * (h % 2), TT * (h % 2) + TT)
                for i, qt in enumerate(Q_TILES):
                    s = TT * (h % 2) + i
                    at_bank, c0 = LOGITS_AT[qt]
                    dve.wait_ge(s_ok, TT * h + (i + 1 if i < 2 else TT))
                    if h >= 2 and i == 0:
                        dve.wait_ge(exp_ok, TT * (h - 1))
                    nc.vector.tensor_reduce(neg_max[:, s:s + 1], bank[at_bank][:, c0:c0 + (qt + 1) * P], AX_X,
                                            ALU.max, negate=True).then_inc(max_ok, 1)
                dve.wait_ge(exp_ok, TT * (h + 1))
                link(nc.vector.reciprocal(p_inv[:, slots], p_sum[:, slots]))
                for i, qt in enumerate(Q_TILES):
                    p = probs[:, P_OFF[qt]:P_OFF[qt] + (qt + 1) * P]
                    s = TT * (h % 2) + i
                    one = ts(p, p, p_inv[:, s:s + 1], None, ALU.mult)
                one.then_inc(p_ok, 1)

            def probs_low(h):
                for i in range(3):
                    dve.wait_ge(pt_hi_ok, 3 * h + i + 1)
                    first, n = ((1, 4), (5, 4), (9, 2))[i]
                    tt(pt_lo[:, first:first + n, :],
                       bank[4 + i][:, 0:n * P].rearrange("p (b c) -> p b c", c=P),
                       pt_hi[:, first:first + n, :], ALU.subtract).then_inc(pt_ok, 1)

            def out_low(h):
                own = slice((h % 2) * HD, (h % 2 + 1) * HD)
                dve.wait_ge(o_hi_ok, h + 1)
                tt(o_lo[own, h // 2, :], bank[7][own, :], o_hi[own, h // 2, :], ALU.subtract).then_inc(o_ok, 1)

            after_block("k", 0)
            make_h(H_Q, 2, lambda j: mcol(1, 0, j), g_hi, g_lo, 0, KT // 2)
            dve.wait_ge(fg_act, 2)
            link(ts(fg_u[:], fg_u[:], 0.0, None, ALU.min))
            nc.vector.tensor_tensor_scan(fg_f[:], fg_l[:], fg_u[:], 0.0, ALU.add, ALU.subtract).then_inc(fg_sum, 1)
            head_norm("k", 0)
            after_block("v", 0)
            make_h(H_Q, 2, lambda j: mcol(1, 0, j), g_hi, g_lo, KT // 2, KT)
            k_low(0)
            after_block("k", 1)
            head_norm("q", 0)
            v_low(0)
            q_low(0)
            q_low(1)
            after_block("q", 0)
            for i in range(KT):
                nxt = i + 1
                softmax(2 * i)
                if i:
                    out_low(2 * i - 1)
                    v_low(i)
                    after_block("v", i)
                else:
                    head_norm("k", 1)
                probs_low(2 * i)
                if nxt < KT:
                    after_block("q", nxt)
                    head_norm("q", nxt)
                softmax(2 * i + 1)
                if i and nxt < KT:
                    head_norm("k", nxt)
                if nxt < KT:
                    q_low(2 * nxt)
                probs_low(2 * i + 1)
                if nxt < KT:
                    k_low(nxt)
                out_low(2 * i)
                if i and nxt < KT:
                    after_block("k", nxt)
                if nxt < KT:
                    q_low(2 * nxt + 1)
            out_low(HEADS - 1)

            dve.wait_ge(normed, 2 * KT)
            dve.wait_ge(v_copied, KT)
            nc.vector.memset(ssum[:], 0.0).then_inc(bank_free, OUT - KVQ)
            dve.wait_ge(bank_free, OUT)
            into_stream(OUT, 3, 1, 2)
            norm_in_halves(3, OUT + KT - 1, H_MLP1, 1, 2, lambda j: gains[:, 3, j:j + 1], lambda j: mcol(1, 3, j))
            mlp(1, MLP1, G_MLP1, True)


_INS = ["x", "c", "ada_w", "ada_b", "norm_mix_g", "norm_mlp_g", "sc_w_in", "sc_conv", "sc_w_out",
        "kv_norm_g", "w_kv", "k_norm_g", "w_f", "b_f", "q_w", "q_norm_g", "o_w", "mlp_w1", "mlp_w2"]


def kernel(**inputs):
    import numpy as np
    import concourse.bacc as bacc
    from concourse.bass_utils import run_bass_kernel_spmd

    nc = bacc.Bacc("TRN2", target_bir_lowering=False, num_devices=1)
    arrays, args = {}, []
    for name in _INS:
        a = np.ascontiguousarray(inputs[name])
        arrays[f"in_{name}"] = a
        args.append(nc.dram_tensor(f"in_{name}", a.shape, mybir.dt.from_np(a.dtype), kind="ExternalInput").ap())
    out = nc.dram_tensor("out", arrays["in_x"].shape, F32, kind="ExternalOutput").ap()
    yoco_trunk(nc, *args, out)
    r = run_bass_kernel_spmd(nc, [arrays], core_ids=[0])
    return r.results[0]["out"]
```
